# Optimizing a Trainium2 kernel written in Bass

```python
import jax
import jax.numpy as jnp
from jax import lax

D_MODEL = 1024
BATCH = 1
SEQ = 512
DEPTH = 2

GLA_HEADS = 4
GLA_DK = 64
GLA_DV = 128
GLA_RANK = 16
GLA_TAU = 16.0
GLA_CHUNK = 64
SWA_HEADS = 8
SWA_KV_HEADS = 2
SWA_HD = 64
WINDOW = 128
ROPE_DIMS = SWA_HD // 4
ROPE_THETA = 500000.0
N_EXPERTS = 16
N_GROUPS = 4
EXPERTS_PER_GROUP = N_EXPERTS // N_GROUPS
TOP_K = 2
D_FF = 512
MOE_BLOCK = 128
EPS = 1e-6
POS_OFFSET_MAX = 1024
IN_WIDTH = 2 * GLA_HEADS * GLA_DK + 2 * GLA_HEADS * GLA_DV + GLA_RANK + SWA_HEADS * SWA_HD + 2 * SWA_KV_HEADS * SWA_HD + 2 * D_MODEL

kernel_name = "hybrid_gla_swa_sink_grouped_moe_adaln"

def rms_norm(x, g):
    xf = x.astype(jnp.float32)
    y = xf * lax.rsqrt(jnp.mean(xf * xf, axis=-1, keepdims=True) + EPS)
    return (y * g).astype(x.dtype)

def partial_rope(x, positions):
    half = ROPE_DIMS // 2
    inv_freq = jnp.power(ROPE_THETA, -jnp.arange(half, dtype=jnp.float32) / half)
    ang = positions.astype(jnp.float32)[..., None] * inv_freq
    cos = jnp.cos(ang)[:, :, None, :]
    sin = jnp.sin(ang)[:, :, None, :]
    xr = x[..., :ROPE_DIMS].astype(jnp.float32)
    x1, x2 = xr[..., :half], xr[..., half:]
    rot = jnp.concatenate([x1 * cos - x2 * sin, x2 * cos + x1 * sin], axis=-1)
    return jnp.concatenate([rot.astype(x.dtype), x[..., ROPE_DIMS:]], axis=-1)

def split_columns(z):
    sizes = (GLA_HEADS * GLA_DK, GLA_HEADS * GLA_DK, GLA_HEADS * GLA_DV, GLA_RANK, GLA_HEADS * GLA_DV,
             SWA_HEADS * SWA_HD, SWA_KV_HEADS * SWA_HD, SWA_KV_HEADS * SWA_HD, D_MODEL, D_MODEL)
    idx, acc = [], 0
    for s in sizes[:-1]:
        acc += s
        idx.append(acc)
    return jnp.split(z, idx, axis=-1)

def gla_branch(q, k, v, a_low, r, w_alpha2, b_alpha, gn_gain):
    B, S, _ = q.shape
    N = S // GLA_CHUNK
    f32 = jnp.float32
    shp_k = (B, N, GLA_CHUNK, GLA_HEADS, GLA_DK)
    shp_v = (B, N, GLA_CHUNK, GLA_HEADS, GLA_DV)
    log_a = jax.nn.log_sigmoid((a_low @ w_alpha2 + b_alpha).astype(f32)) / GLA_TAU
    b = jnp.cumsum(log_a.reshape(shp_k), axis=2)
    q = q.astype(f32).reshape(shp_k) * (GLA_DK ** -0.5)
    k = k.astype(f32).reshape(shp_k)
    v = v.astype(f32).reshape(shp_v)
    q_dec = q * jnp.exp(b)
    k_inv = k * jnp.exp(-b)
    causal = jnp.tril(jnp.ones((GLA_CHUNK, GLA_CHUNK), dtype=bool))
    att = jnp.where(causal, jnp.einsum('bnihd,bnjhd->bnhij', q_dec, k_inv), 0.0)
    o_intra = jnp.einsum('bnhij,bnjhe->bnihe', att, v)
    b_end = b[:, :, -1]
    k_end = k * jnp.exp(b_end[:, :, None] - b)
    kv = jnp.einsum('bnjhd,bnjhe->nbhde', k_end, v)

    def step(state, inp):
        decay, kv_n = inp
        return decay[..., None] * state + kv_n, state

    s0 = jnp.zeros((B, GLA_HEADS, GLA_DK, GLA_DV), f32)
    _, s_prev = lax.scan(step, s0, (jnp.exp(b_end).transpose(1, 0, 2, 3), kv))
    o_inter = jnp.einsum('bnihd,nbhde->bnihe', q_dec, s_prev)
    o = (o_intra + o_inter).reshape(B, S, GLA_HEADS, GLA_DV)
    o = rms_norm(o, gn_gain.reshape(GLA_HEADS, GLA_DV))
    return (o.reshape(B, S, GLA_HEADS * GLA_DV) * jax.nn.silu(r.astype(f32))).astype(r.dtype)

def swa_branch(q, k, v, positions, qn_gain, kn_gain, sinks):
    B, S, _ = q.shape
    N = S // WINDOW
    G = SWA_HEADS // SWA_KV_HEADS
    q = partial_rope(rms_norm(q.reshape(B, S, SWA_HEADS, SWA_HD), qn_gain), positions)
    k = partial_rope(rms_norm(k.reshape(B, S, SWA_KV_HEADS, SWA_HD), kn_gain), positions)
    v = v.reshape(B, S, SWA_KV_HEADS, SWA_HD)
    qb = q.reshape(B, N, WINDOW, SWA_KV_HEADS, G, SWA_HD)
    kb = k.reshape(B, N, WINDOW, SWA_KV_HEADS, SWA_HD)
    vb = v.reshape(B, N, WINDOW, SWA_KV_HEADS, SWA_HD)
    pad = ((0, 0), (1, 0), (0, 0), (0, 0), (0, 0))
    k_band = jnp.concatenate([jnp.pad(kb[:, :-1], pad), kb], axis=2)
    v_band = jnp.concatenate([jnp.pad(vb[:, :-1], pad), vb], axis=2)
    s = jnp.einsum('bnikgd,bnjkd->bnkgij', qb, k_band).astype(jnp.float32) * (SWA_HD ** -0.5)
    i = jnp.arange(WINDOW)[:, None]
    j = jnp.arange(2 * WINDOW)[None, :]
    band = (j > i) & (j <= i + WINDOW)
    valid = band[None] & ((jnp.arange(N)[:, None, None] > 0) | (j >= WINDOW)[None])
    s = jnp.where(valid[None, :, None, None], s, jnp.float32(-1e30))
    sink = sinks.astype(jnp.float32).reshape(SWA_KV_HEADS, G)[None, None, :, :, None, None]
    m = jnp.maximum(jnp.max(s, axis=-1, keepdims=True), sink)
    p = jnp.exp(s - m)
    p = p / (jnp.sum(p, axis=-1, keepdims=True) + jnp.exp(sink - m))
    o = jnp.einsum('bnkgij,bnjkd->bnikgd', p.astype(v.dtype), v_band)
    return o.reshape(B, S, SWA_HEADS * SWA_HD)

def group_limited_route(h, w_router, b_router):
    aff = jax.nn.sigmoid((h @ w_router).astype(jnp.float32))
    sel = (aff + b_router.astype(jnp.float32)).reshape(-1, N_GROUPS, EXPERTS_PER_GROUP)
    group_score = lax.top_k(sel, TOP_K)[0].sum(-1)
    group = jnp.argmax(group_score, axis=-1)
    in_group = jnp.take_along_axis(sel, group[:, None, None], axis=1)[:, 0]
    _, local = lax.top_k(in_group, TOP_K)
    expert = (group[:, None] * EXPERTS_PER_GROUP + local).astype(jnp.int32)
    w = jnp.take_along_axis(aff, expert, axis=1)
    return expert, w / jnp.sum(w, axis=-1, keepdims=True)

def moe_ffn(h, w_router, b_router, w_gate, w_up, w_down):
    T, D = h.shape
    expert, weight = group_limited_route(h, w_router, b_router)
    A = T * TOP_K
    e_flat = expert.reshape(A)
    tok_flat = jnp.repeat(jnp.arange(T, dtype=jnp.int32), TOP_K)
    order = jnp.argsort(e_flat)
    e_s = e_flat[order]
    tok_s = tok_flat[order]
    w_s = weight.reshape(A)[order]
    counts = jnp.bincount(e_flat, length=N_EXPERTS)
    starts = jnp.cumsum(counts) - counts
    padded = (counts + MOE_BLOCK - 1) // MOE_BLOCK * MOE_BLOCK
    pad_end = jnp.cumsum(padded)
    dest = pad_end[e_s] - padded[e_s] + jnp.arange(A, dtype=jnp.int32) - starts[e_s]
    n_blocks = -(-A // MOE_BLOCK) + N_EXPERTS
    slots = n_blocks * MOE_BLOCK
    tok_buf = jnp.zeros((slots,), jnp.int32).at[dest].set(tok_s)
    w_buf = jnp.zeros((slots,), jnp.float32).at[dest].set(w_s)
    blk_start = jnp.arange(n_blocks, dtype=jnp.int32) * MOE_BLOCK
    blk_exp = jnp.minimum(jnp.searchsorted(pad_end, blk_start, side='right'), N_EXPERTS - 1)

    def expert_block(args):
        tok, e = args
        xb = h[tok]
        return (jax.nn.silu(xb @ w_gate[e]) * (xb @ w_up[e])) @ w_down[e]

    y = lax.map(expert_block, (tok_buf.reshape(n_blocks, MOE_BLOCK), blk_exp))
    contrib = y.reshape(slots, D) * w_buf[:, None].astype(h.dtype)
    return jnp.zeros_like(h).at[tok_buf].add(contrib)

def setup_inputs(seed: int = 0) -> dict:
    key = jax.random.key(seed)
    ks = jax.random.split(key, 24)
    f32 = jnp.float32
    L, D = DEPTH, D_MODEL

    def nrm(k, shape, scale):
        return jax.random.normal(k, shape, f32) * scale

    offsets = jax.random.randint(ks[2], (BATCH, 1), 0, POS_OFFSET_MAX, dtype=jnp.int32)
    return {
        'x': nrm(ks[0], (BATCH, SEQ, D), 1.0),
        'c': nrm(ks[1], (BATCH, D), 1.0),
        'positions': offsets + jnp.arange(SEQ, dtype=jnp.int32)[None, :],
        'w_ada': nrm(ks[3], (L, D, 6 * D), 0.5 * D ** -0.5),
        'b_ada': nrm(ks[4], (L, 6 * D), 0.02),
        'norm_mix': 1.0 + nrm(ks[5], (L, D), 0.05),
        'w_in': nrm(ks[6], (L, D, IN_WIDTH), D ** -0.5),
        'w_alpha2': nrm(ks[7], (L, GLA_RANK, GLA_HEADS * GLA_DK), GLA_RANK ** -0.5),
        'b_alpha': nrm(ks[8], (L, GLA_HEADS * GLA_DK), 0.02),
        'gla_norm': 1.0 + nrm(ks[9], (L, GLA_HEADS * GLA_DV), 0.05),
        'q_norm': 1.0 + nrm(ks[10], (L, SWA_HD), 0.05),
        'k_norm': 1.0 + nrm(ks[11], (L, SWA_HD), 0.05),
        'sinks': nrm(ks[12], (L, SWA_HEADS), 0.5),
        'w_up_gla': nrm(ks[13], (L, GLA_HEADS * GLA_DV, D), (GLA_HEADS * GLA_DV) ** -0.5),
        'w_up_swa': nrm(ks[14], (L, SWA_HEADS * SWA_HD, D), (SWA_HEADS * SWA_HD) ** -0.5),
        'w_out': nrm(ks[15], (L, D, D), D ** -0.5),
        'norm_ffn': 1.0 + nrm(ks[16], (L, D), 0.05),
        'w_router': nrm(ks[17], (D, N_EXPERTS), D ** -0.5),
        'b_router': nrm(ks[18], (N_EXPERTS,), 0.01),
        'w_gate': nrm(ks[19], (L, N_EXPERTS, D, D_FF), D ** -0.5),
        'w_up': nrm(ks[20], (L, N_EXPERTS, D, D_FF), D ** -0.5),
        'w_down': nrm(ks[21], (L, N_EXPERTS, D_FF, D), D_FF ** -0.5),
    }

def reference(x, c, positions, w_ada, b_ada, norm_mix, w_in, w_alpha2, b_alpha, gla_norm,
              q_norm, k_norm, sinks, w_up_gla, w_up_swa, w_out, norm_ffn, w_router, b_router,
              w_gate, w_up, w_down):
    B, S, D = x.shape
    cond = jax.nn.silu(c)
    for l in range(DEPTH):
        mod = cond @ w_ada[l] + b_ada[l]
        sh1, sc1, g1, sh2, sc2, g2 = [m[:, None, :] for m in jnp.split(mod, 6, axis=-1)]
        h = rms_norm(x, norm_mix[l]) * (1.0 + sc1) + sh1
        gq, gk, gv, ga, gr, sq, sk, sv, mix_a, mix_b = split_columns(h @ w_in[l])
        y_gla = gla_branch(gq, gk, gv, ga, gr, w_alpha2[l], b_alpha[l], gla_norm[l]) @ w_up_gla[l]
        y_swa = swa_branch(sq, sk, sv, positions, q_norm[l], k_norm[l], sinks[l]) @ w_up_swa[l]
        merged = jax.nn.sigmoid(mix_a) * y_gla + jax.nn.sigmoid(mix_b) * y_swa
        x = x + g1 * (merged @ w_out[l])
        h2 = rms_norm(x, norm_ffn[l]) * (1.0 + sc2) + sh2
        y = moe_ffn(h2.reshape(B * S, D), w_router, b_router, w_gate[l], w_up[l], w_down[l])
        x = x + g2 * y.reshape(B, S, D)
    return x


_drawn_inputs = setup_inputs


def setup_inputs(seed=0):
    import zlib

    import numpy as np

    out = dict(_drawn_inputs(seed))
    spreads = {}
    factors = {'b_alpha': 8.0, 'q_norm': 4.617, 'k_norm': 4.507, 'sinks': 45.072}
    for name, (base, spread) in spreads.items():
        noise = np.random.default_rng([zlib.crc32(name.encode()), seed]).standard_normal(out[name].shape)
        drawn = base * np.exp(spread * noise) if base else spread * noise
        out[name] = jnp.asarray(drawn.astype(out[name].dtype))
    for name, factor in factors.items():
        out[name] = (out[name] * factor).astype(out[name].dtype)
    return out
```

```python
from contextlib import ExitStack

import numpy as np
import concourse.bass as bass
from concourse import mybir

F32 = mybir.dt.float32
I32 = mybir.dt.int32
U32 = mybir.dt.uint32
ACT = mybir.ActivationFunctionType
ALU = mybir.AluOpType
AX = mybir.AxisListType

P = 128
EPS = 1e-6
NEG = -1e30
GLA_TAU = 16.0
GLA_RANK = 16
CHUNK = 64
ROPE_THETA = 500000.0
SLOTS = 6
MASK = 13


def trunk(nc, x, c, positions, w_ada, b_ada, norm_mix, w_in, w_alpha2, b_alpha, gla_norm,
          q_norm, k_norm, sinks, w_up_gla, w_up_swa, w_out, norm_ffn, w_router, b_router,
          w_gate, w_up, w_down, out):
    _, SEQ, D = x.shape
    DEPTH = w_ada.shape[0]
    NT = SEQ // P
    C = D // P
    E = w_router.shape[1]
    FF = w_gate.shape[3]
    FC = FF // P
    HD = q_norm.shape[1]
    QH = sinks.shape[1]
    KVH = 2
    GW = w_alpha2.shape[2]
    GV = gla_norm.shape[1]
    GH = GW // HD
    NCH = SEQ // CHUNK
    G4 = 4
    HALF = HD // 8
    NN = QH + KVH
    TOPK = 2
    col_qk, col_v = 0, 2 * GW
    col_a = col_v + GV
    col_r = col_a + GLA_RANK
    col_sq = col_r + GV
    col_sk = col_sq + QH * HD
    col_ma = col_sk + 2 * KVH * HD
    col_mb = col_ma + D

    ADA = 6 * D // 512
    U_QK, U_V, U_R, U_SQ, U_MA0, U_MB0, U_UPG, U_UPS, U_MA1, U_MB1, U_O0, U_O1 = range(ADA, ADA + 12)
    U_MOE = ADA + 12
    UNITS = U_MOE + 3 * E
    assert UNITS % SLOTS == 0 and U_MOE % SLOTS == 0
    PER_SLOT = UNITS // SLOTS

    R_SH1, R_SC1, R_G1, R_SH2, R_SC2, R_G2, R_NM = (C * i for i in range(7))
    R_NF = R_NM + C
    R_BA = R_NF + C
    R_GN = R_BA + GW // P
    R_END = R_GN + GV // P

    def dram(name, shape, dt=F32):
        return nc.dram_tensor(name, shape, dt, kind="Internal").ap()

    xs_rows = dram("xs_rows", (SEQ, D))
    y_rows = dram("y_rows", (TOPK * SEQ, D))
    slot_table = dram("slot_table", (P * G4 * E, 1), I32)

    with ExitStack() as ctx:
        def sb(name, shape, dt=F32):
            return ctx.enter_context(nc.sbuf_tensor(name, shape, dt))

        def sem(name):
            return ctx.enter_context(nc.semaphore(name))

        ring = sb("ring", [P, SLOTS, 4096])
        xt = sb("xt", [P, NT, D])
        hT = sb("hT", [P, C, SEQ])
        w_a = sb("w_a", [P, C, GLA_RANK])
        grow = sb("grow", [P, D])
        reg0 = sb("reg0", [P, 4096])
        reg1 = sb("reg1", [P, 2048])
        reg23 = sb("reg23", [P, 4096])
        reg4 = sb("reg4", [P, 2048])
        reg5 = sb("reg5", [P, 2048])
        reg6 = sb("reg6", [P, NT * NN * HD])
        reg7 = sb("reg7", [P, 1024])
        v_tm = sb("v_tm", [P, NT, KVH * HD])
        ident = sb("ident", [P, P])
        ones = sb("ones", [P, P])
        before = sb("before", [P, P])
        causal = sb("causal", [P, P])
        band = sb("band", [P, 2 * P])
        cosr = sb("cosr", [P, NT, HALF])
        sinr = sb("sinr", [P, NT, HALF])
        pcs = sb("pcs", [P, DEPTH, R_END])
        pc = sb("pc", [P, R_END])
        a1 = sb("a1", [P, C])
        a2 = sb("a2", [P, C])
        condT = sb("condT", [P, C])
        gains = sb("gains", [P, 2, HD])
        sink_t = sb("sink_t", [P, QH])
        wr = sb("wr", [P, C, E])
        br = sb("br", [P, E])
        ss = sb("ss", [P, NT])
        rstd = sb("rstd", [P, NT])
        qss = sb("qss", [P, NT, NN])
        decay = sb("decay", [P, 2, NCH])
        smax = sb("smax", [P, QH])
        nmax = sb("nmax", [P, 2, QH])
        ssum = sb("ssum", [P, 2, QH])
        snk = sb("snk", [P, 2, QH])
        cst = sb("cst", [P, 4])
        wg4 = sb("wg4", [P, G4])
        w16 = sb("w16", [P, E])
        e4 = sb("e4", [P, E])
        wts = sb("wts", [P, TOPK, NT])
        row_i = sb("row_i", [P, TOPK * NT], I32)
        ids = sb("ids", [P, TOPK * NT], I32)
        table = sb("table", [P, G4 * E], I32)
        gidx = sb("gidx", [P, G4 * E], I32)
        no_slot = sb("no_slot", [P, G4 * E], I32)
        cnt_i = sb("cnt_i", [P, E], I32)
        icur = sb("icur", [P, 8], I32)
        posi = sb("posi", [P, NT], I32)
        PS = ctx.enter_context(nc.psum_tensor("PS", [P, 8, 512], F32))

        xs = reg0[:, :].rearrange("p (t d) -> p t d", t=NT)
        la = reg0[:, 0:1024].rearrange("p (m s) -> p m s", m=2)
        bb = reg0[:, 1024:2048].rearrange("p (m s) -> p m s", m=2)
        qdec = reg0[:, 2048:3072].rearrange("p (m s) -> p m s", m=2)
        kinv = reg0[:, 3072:4096].rearrange("p (m s) -> p m s", m=2)
        kend = reg1[:, 0:1024].rearrange("p (m s) -> p m s", m=2)
        kend_tm = reg1[:, 1024:2048].rearrange("p (t n) -> p t n", t=NT)
        v = reg23[:, 0:2048].rearrange("p (t n) -> p t n", t=NT)
        S = reg23[:, 2048:4096].rearrange("p (m n e) -> p m n e", m=2, n=NCH)
        rs = reg4[:, :].rearrange("p (h s) -> p h s", h=GH)
        w_kv = reg5[:, :].rearrange("p (c n) -> p c n", c=C)
        attm = reg5[:, 0:2 * SEQ].rearrange("p (i t s) -> p i t s", i=2, t=NT)
        ada_acc = [reg6[:, 1024 + 512 * i:1536 + 512 * i] for i in range(2)]
        params = reg4[0:R_END, 0:DEPTH * P].rearrange("p (l n) -> p l n", l=DEPTH)
        scanm = reg6[:, 0:SEQ]
        rt = reg1[:, 0:20 * NT * E].rearrange("p (a n) -> p a n", n=NT * E)
        crow = reg7[0:C, 0:P]
        walpha = reg7[0:GLA_RANK, 512:512 + GW]
        aT = reg7[0:GLA_RANK, 0:512]
        osq = reg7[:, 0:512]
        orr = reg7[:, 512:1024]
        qk = reg6[:, :].rearrange("p (t h d) -> p t h d", t=NT, h=NN)
        sqt = reg1[:, 0:1280]
        qT = reg0[:, 0:2048].rearrange("p (a s) -> p a s", a=QH // 2)
        oTs = reg0[:, 2048:4096].rearrange("p (a s) -> p a s", a=QH // 2)
        kT = reg1[:, 0:1024].rearrange("p (g s) -> p g s", g=KVH)
        kd = reg1[:, 1024:2048].rearrange("p (t g r d) -> p t g r d", t=NT, g=KVH, r=2)
        pT = reg23[:, 0:2048].rearrange("p (b j s) -> p b j s", b=2, j=QH)
        sc = [reg6[:, 0:2048].rearrange("p (j s) -> p j s", j=QH),
              reg23[:, 2048:4096].rearrange("p (j s) -> p j s", j=QH)]
        sig = [reg6[:, 1024 * i:1024 * i + 1024].rearrange("p (a s) -> p a s", a=2) for i in range(2)]
        mT = reg23[:, :].rearrange("p (j s) -> p j s", j=C)
        otmp = [reg6[:, 512 * i:512 * i + 512] for i in range(2)]
        diag = reg4[:, 0:1024].rearrange("p (c n) -> p c n", c=C)
        xg = [reg23[:, 1024 * i:1024 * i + 1024] for i in range(2)]
        xgT = [reg23[:, 2048 + 1024 * i:3072 + 1024 * i].rearrange("p (c s) -> p c s", c=C) for i in range(2)]
        msig = [reg1[:, 512 * i:512 * i + 512] for i in range(2)]
        mact = [reg1[:, 1024 + 512 * i:1536 + 512 * i] for i in range(2)]
        maT = [reg7[:, 512 * i:512 * i + 512].rearrange("p (f s) -> p f s", f=FC) for i in range(2)]
        ysb = [reg5[:, 1024 * i:1024 * i + 1024] for i in range(2)]
        yc = [reg0[:, 2048 * i:2048 * i + 2048].rearrange("p (k d) -> p k d", k=TOPK) for i in range(2)]
        hflat = hT[:, :, :].rearrange("p c s -> p (c s)")
        o_xg = hflat[:, 0:1024]
        o_xgT = hflat[:, 1024:2048].rearrange("p (c s) -> p c s", c=C)
        o_sig = hflat[:, 2048:2560]
        o_act = hflat[:, 2560:3072]
        o_aT = hflat[:, 3072:3584].rearrange("p (f s) -> p f s", f=FC)
        o_ysb = reg6[:, 0:1024]

        def slot(u, n=C):
            return ring[:, u % SLOTS, :].rearrange("p (c n) -> p c n", c=n)

        K = {}

        def counted(name, k):
            s = sem(name)
            K[s.name] = k
            return s

        def at(s, l, k):
            return l * K[s.name] + k

        loaded = [counted(f"slot{i}_loaded", 16 * PER_SLOT) for i in range(SLOTS)]
        small_loaded = counted("small_weights_loaded", 32)
        par_loaded = counted("small_params_loaded", 16 * 4)
        ada_ready = counted("ada_products_ready", ADA)
        ada_summed = counted("ada_columns_ready", ADA)
        diag_done = counted("gate_diagonal_built", 2)
        grow_ready = counted("gate_rows_ready", 2)
        grow_done = counted("gate_rows_copied", 2)
        root = counted("token_rms_rooted", 2)
        xs_ready = counted("xs_ready", 8)
        ht_ready = counted("hT_ready", 16)
        ht_done = counted("hT_copied", 16)
        scanm_made = counted("scan_mask_made", 2)
        a_ready = counted("alow_ready", 1)
        a_done = counted("alow_copied", 1)
        v_ready = counted("v_ready", NT)
        v_done = counted("v_copied", NT)
        u_ready = counted("alpha_ready", 2)
        u_done = counted("alpha_copied", 2)
        labs = counted("alpha_abs_taken", 1)
        lln = counted("log_term_ready", 1)
        b_done = counted("cumsum_ready", 1)
        dif_done = counted("decay_to_end_ready", 1)
        eplus = counted("exponents_ready", 1)
        eend = counted("end_exponents_ready", 1)
        qk_ready = counted("gla_qk_ready", 4)
        qk_done = counted("gla_qk_decayed", 3)
        r_ready = counted("r_ready", 4)
        r_sig = counted("r_sigmoid_ready", 4)
        r_done = counted("r_gated", 4)
        sq_ready = counted("swa_q_ready", NT)
        sq_done = counted("swa_q_copied", NT)
        skv_ready = counted("swa_kv_ready", NT)
        skv_done = counted("swa_kv_copied", NT)
        kt_ready = counted("kend_transposed", 2)
        kt_done = counted("kend_copied", 2)
        kv_ready = counted("kv_ready", 4)
        s_done = counted("states_ready", 1)
        att_ready = counted("att_ready", GH)
        att_done = counted("att_masked", GH)
        o_ready = counted("gla_o_ready", GH)
        osq_done = counted("gla_o_squared", GH)
        ms_ready = counted("gla_mean_square_ready", GH)
        orr_done = counted("gla_root_ready", GH)
        o_done = counted("gla_o_done", GH)
        qsq_done = counted("swa_squares_ready", 2)
        qss_done = counted("swa_square_sums_ready", 2)
        qrt_done = counted("swa_roots_ready", 1)
        rope_done = counted("swa_rotated", 1)
        qT_ready = counted("swa_qT_ready", NT)
        kT_ready = counted("swa_kT_ready", NT)
        qT_done = counted("swa_qT_copied", NT)
        kT_done = counted("swa_kT_copied", NT)
        sc_ready = counted("scores_ready", NT)
        sc_read = counted("scores_read", NT)
        max_done = counted("score_max_ready", NT)
        p_exp = counted("probs_ready", NT)
        p_done = counted("probs_normed", NT)
        pTa_ready = counted("probs_T_ready_act", NT * 2 - 1)
        pTd_ready = counted("probs_T_ready_dve", NT * 2 - 1)
        pTa_done = counted("probs_T_copied_act", NT * 2 - 1)
        pTd_done = counted("probs_T_copied_dve", NT * 2 - 1)
        pv_ready = counted("swa_o_ready", NT)
        pv_done = counted("swa_o_copied", NT)
        mx_ready = counted("mix_products_ready", 4 * C)
        mx_sig = counted("mix_sigmoids_ready", 2 * C)
        mx_done = counted("merged", C)
        out_ready = counted("out_products_ready", 2 * NT)
        x_done = counted("residual_added", 2 * NT)
        xs_out = counted("xs_rows_written", 16)
        lg_ready = counted("logits_ready", 1)
        aff_done = counted("affinities_ready", 1)
        m_done = counted("choice_mask_ready", 1)
        rk_ready = counted("ranks_ready", 1)
        row_done = counted("table_rows_ready", 1)
        tab_clear = counted("table_cleared", 16)
        tab_set = counted("table_filled", 16 * TOPK * NT)
        tab_loaded = counted("table_loaded", 16)
        idx_done = counted("gather_rows_ready", 1)
        gcur_done = counted("gather_column_copied", E)
        dcur_done = counted("scatter_column_copied", E)
        xg_loaded = [counted(f"expert_tokens_gathered_{i}", 8 * E) for i in range(2)]
        t1_ready = counted("expert_tokens_transposed", E)
        t1_done = counted("expert_tokens_copied", E)
        g_ready = counted("gate_product_ready", E)
        u2_ready = counted("up_product_ready", E)
        gu_free = counted("gate_up_weights_free", E)
        sig_done = counted("gate_sigmoid_ready", E)
        act_done = counted("expert_act_ready", E)
        t2_ready = counted("expert_act_transposed", E)
        t2_done = counted("expert_act_copied", E)
        d_ready = counted("down_product_ready", E)
        y_done = counted("expert_y_ready", E + 1)
        y_stored = [counted(f"expert_y_scattered_{i}", 8 * E) for i in range(2)]
        yc_loaded = [counted(f"chosen_y_loaded_{i}", 8 * NT) for i in range(2)]
        x2_done = counted("moe_added", NT)
        x_loaded = sem("x_loaded")
        const_loaded = sem("constants_loaded")
        pool_consts = sem("pool_constants")
        dve_consts = sem("dve_constants")
        trig = sem("trig_steps")
        trig_act = sem("trig_functions")
        cond_t = sem("condition_transposed")
        pcs_ready = sem("parameters_transposed")
        cond_sig = sem("condition_sigmoid")
        cond_done = sem("condition_ready")
        x_stored = sem("x_stored")
        o_icur = sem("ovf_index_copied")
        o_gath = sem("ovf_gathered")
        o_t1 = sem("ovf_tokens_transposed")
        o_t1c = sem("ovf_tokens_copied")
        o_gu = sem("ovf_gate_up_ready")
        o_sg = sem("ovf_sigmoid_ready")
        o_ac = sem("ovf_act_ready")
        o_t2 = sem("ovf_act_transposed")
        o_t2c = sem("ovf_act_copied")
        o_d = sem("ovf_down_ready")
        o_y = sem("ovf_y_ready")
        o_st = sem("ovf_scattered")

        block = ctx.enter_context(nc.Block())

        def overflow_blocks(eng, e, done, body):
            count = eng.value_load(cnt_i[0:1, bass.ds(e, 1)], min_val=0, max_val=SEQ)
            for b in range(1, NT):
                with eng.If(count > P * b):
                    eng.reg_add(done, done, 1)
                    body(b, eng.snap(done, min_val=1, max_val=4096))
                    eng.nop()

        @block.sync
        def _(sp):
            def load(l, u):
                if u < ADA:
                    src = w_ada[l, :, 512 * u:512 * u + 512].rearrange("(c p) n -> p c n", p=P)
                elif u in (U_UPG, U_UPS):
                    w = w_up_gla if u == U_UPG else w_up_swa
                    src = w[l].rearrange("(c p) n -> p c n", p=P)
                elif u in (U_O0, U_O1):
                    h = 512 * (u - U_O0)
                    src = w_out[l, :, h:h + 512].rearrange("(c p) n -> p c n", p=P)
                else:
                    at_col = {U_QK: col_qk, U_V: col_v, U_R: col_r, U_SQ: col_sq, U_MA0: col_ma,
                              U_MB0: col_mb, U_MA1: col_ma + 512, U_MB1: col_mb + 512}[u]
                    src = w_in[l, :, at_col:at_col + 512].rearrange("(c p) n -> p c n", p=P)
                sp.dma_start(slot(u, src.shape[1]), src).then_inc(loaded[u % SLOTS], 16)

            def load_expert(l, e, k, part):
                u = U_MOE + 3 * k + part
                src = (w_gate, w_up, w_down)[part][l, e].rearrange("(c p) n -> p c n", p=P)
                sp.dma_start(slot(u, src.shape[1]), src).then_inc(loaded[u % SLOTS], 16)

            sp.dma_start(xt[:, :, :], x[0].rearrange("(t p) d -> p t d", p=P)).then_inc(x_loaded, 16)
            sp.dma_start(crow, c.rearrange("b (c p) -> (b c) p", p=P)).then_inc(const_loaded, 16)
            sp.dma_start(posi[:, :], positions.rearrange("b (t p) -> p (b t)", p=P),
                         allow_slow_non_contiguous=True).then_inc(const_loaded, 16)
            sp.dma_start(wr[:, :, :], w_router.rearrange("(c p) e -> p c e", p=P)).then_inc(const_loaded, 16)
            sp.dma_start(br[:, :], b_router.rearrange("(a e) -> a e", a=1).broadcast_to([P, E])).then_inc(const_loaded, 16)
            for a, b, src in ((R_SH1, R_NM, b_ada), (R_NM, R_NF, norm_mix), (R_NF, R_BA, norm_ffn),
                              (R_BA, R_GN, b_alpha), (R_GN, R_END, gla_norm)):
                sp.dma_start(params[a:b, :, :], src.rearrange("l (c p) -> c l p", p=P)).then_inc(const_loaded, 16)
            for u in range(SLOTS):
                load(0, u)
            number = sp.alloc_register("sp_wait_value")

            def in_register(value):
                sp.reg_mov(number, value)
                return sp.snap(number, min_val=1, max_val=1 << 14)

            free = {u: (ada_ready, u + 1) for u in range(ADA)}
            free |= {U_QK: (qk_ready, 4), U_V: (v_ready, NT), U_R: (r_ready, 4), U_SQ: (sq_ready, NT),
                     U_MA0: (mx_ready, 2 * C - 3), U_MB0: (mx_ready, 2 * C - 2),
                     U_UPG: (mx_ready, 4 * C - 1), U_UPS: (mx_ready, 4 * C),
                     U_MA1: (mx_ready, 4 * C - 3), U_MB1: (mx_ready, 4 * C - 2),
                     U_O0: (out_ready, NT), U_O1: (out_ready, 2 * NT)}
            with sp.Fori(0, DEPTH) as l:
                sp.dma_start(w_a[:, :, :], w_in[l, :, col_a:col_a + GLA_RANK].rearrange("(c p) n -> p c n", p=P)).then_inc(small_loaded, 16)
                for u in range(U_MOE):
                    s, k = free[u]
                    value = in_register(at(s, l, k))
                    sp.wait_ge(x_loaded, 16)
                    sp.wait_ge(s, value)
                    if u == U_QK:
                        sp.dma_start(w_kv, w_in[l, :, col_sk:col_ma].rearrange("(c p) n -> p c n", p=P)).then_inc(small_loaded, 16)
                    n = u + SLOTS
                    if n < U_MOE:
                        load(l, n)
                    else:
                        load_expert(l, (n - U_MOE) // 3, (n - U_MOE) // 3, (n - U_MOE) % 3)
                with sp.Fori(0, E // 2 - 1) as j:
                    for k in range(2):
                        for part in range(3):
                            s = d_ready if part == 2 else gu_free
                            sp.wait_ge(s, at(s, l, 2 * j + k + 1))
                            load_expert(l, 2 * j + (k + 2), k, part)
                with sp.If(l < DEPTH - 1):
                    following = nc.s_assert_within(l + 1, 1, DEPTH - 1, skip_runtime_bounds_check_because="the If above bounds it")
                    for u in range(SLOTS):
                        s = d_ready if u % 3 == 2 else gu_free
                        sp.wait_ge(s, at(s, l, E - 1 + u // 3))
                        load(following, u)
                sp.nop()
            for t in range(NT):
                sp.wait_ge(x2_done, at(x2_done, DEPTH - 1, t + 1))
                sp.dma_start(out[0, t * P:t * P + P, :], xt[:, t, :]).then_inc(x_stored, 16)
            sp.wait_ge(x_stored, 16 * NT)

        @block.gpsimd
        def _(pool):
            pool.memset(ident[:, :], 0.0).then_inc(pool_consts, 1)
            pool.memset(ones[:, :], 1.0).then_inc(pool_consts, 1)
            pool.memset(band[:, :], 0.0).then_inc(pool_consts, 1)
            pool.memset(no_slot[:, :], 4 * SEQ).then_inc(pool_consts, 1)
            pool.iota(ids[:, :].rearrange("p (k t) -> p k t", k=TOPK), [[1, TOPK], [2 * P, NT]], base=0,
                      channel_multiplier=2).then_inc(pool_consts, 1)
            pool.wait_ge(pool_consts, 5)
            pool.affine_select(out=ident[:, :], in_=ident[:, :], compare_op=ALU.not_equal, fill=1.0, base=0,
                               pattern=[[-1, P]], channel_multiplier=1).then_inc(pool_consts, 1)
            pool.affine_select(out=before[:, :], in_=ones[:, :], compare_op=ALU.is_gt, fill=0.0, base=0,
                               pattern=[[1, P]], channel_multiplier=-1).then_inc(pool_consts, 1)
            pool.affine_select(out=causal[:, :], in_=ones[:, :], compare_op=ALU.is_ge, fill=0.0, base=0,
                               pattern=[[1, P]], channel_multiplier=-1).then_inc(pool_consts, 1)
            pool.affine_select(out=band[:, :], in_=band[:, :], compare_op=ALU.is_gt, fill=NEG, base=0,
                               pattern=[[1, 2 * P]], channel_multiplier=-1).then_inc(pool_consts, 1)
            pool.wait_ge(pool_consts, 9)
            pool.affine_select(out=band[:, :], in_=band[:, :], compare_op=ALU.is_ge, fill=NEG, base=P,
                               pattern=[[-1, 2 * P]], channel_multiplier=1).then_inc(pool_consts, 1)
            pool.memset(causal[0:CHUNK, CHUNK:P], 0.0).then_inc(pool_consts, 1)
            for tile, pattern, base in ((wg4, [[-1, G4]], G4), (w16, [[-1, E]], E), (e4, [[G4, E]], 0)):
                pool.iota(tile[:, :], pattern, base=base, channel_multiplier=0,
                          allow_small_or_imprecise_dtypes=True).then_inc(pool_consts, 1)

            done = pool.alloc_register("pool_ovf")
            pool.reg_mov(done, 0)
            number = pool.alloc_register("pool_wait_value")

            def in_register(value):
                pool.reg_mov(number, value)
                return pool.snap(number, min_val=1, max_val=1 << 14)

            pool.wait_ge(const_loaded, 16 * 9)

            with pool.Fori(0, DEPTH) as l:
                pool.dma_start(walpha, w_alpha2[l]).then_inc(par_loaded, 16)
                pool.dma_start(gains[:, 0, :], q_norm[bass.ds(l, 1), :].broadcast_to([P, HD])).then_inc(par_loaded, 16)
                pool.dma_start(gains[:, 1, :], k_norm[bass.ds(l, 1), :].broadcast_to([P, HD])).then_inc(par_loaded, 16)
                pool.memset(scanm, 1.0).then_inc(scanm_made, 1)
                value = in_register(at(scanm_made, l, 1))
                pool.wait_ge(pool_consts, 14)
                pool.wait_ge(scanm_made, value)
                pool.memset(scanm.rearrange("p (n s) -> p n s", s=CHUNK)[:, :, 0:1], 0.0).then_inc(scanm_made, 1)
                pool.dma_start(sink_t[:, :], sinks[bass.ds(l, 1), :].broadcast_to([P, QH])).then_inc(par_loaded, 16)
                pool.dma_start(slot_table.rearrange("(p n) a -> p (n a)", p=P), no_slot[:, :]).then_inc(tab_clear, 16)
                value = in_register(at(xs_ready, l, 2 * NT))
                pool.wait_ge(pool_consts, 14)
                pool.wait_ge(xs_ready, value)
                pool.dma_start(xs_rows.rearrange("(t p) d -> p t d", p=P), xs).then_inc(xs_out, 16)
                values = [in_register(at(tab_clear, l, 16)), in_register(at(row_done, l, 1))]
                pool.wait_ge(pool_consts, 14)
                pool.wait_ge(tab_clear, values[0])
                pool.wait_ge(row_done, values[1])
                for i in range(TOPK * NT):
                    pool.indirect_dma_start(out=slot_table[:, :], out_offset=bass.IndirectOffsetOnAxis(
                        ap=row_i[:, i:i + 1].bitcast(U32), axis=0), in_=ids[:, i:i + 1], in_offset=None).then_inc(tab_set, 16)
                value = in_register(at(tab_set, l, 16 * TOPK * NT))
                pool.wait_ge(pool_consts, 14)
                pool.wait_ge(tab_set, value)
                pool.dma_start(table[:, :], slot_table.rearrange("(p n) a -> p (n a)", p=P)).then_inc(tab_loaded, 16)
                values = [in_register(at(idx_done, l, 1)), in_register(at(xs_out, l, 16))]
                pool.wait_ge(pool_consts, 14)
                pool.wait_ge(idx_done, values[0])
                pool.wait_ge(xs_out, values[1])

                def gather(e, k):
                    pool.tensor_copy(icur[:, k:k + 1], gidx[:, bass.ds(e * G4, 1)]).then_inc(gcur_done, 1)
                    value = in_register(at(gcur_done, l, e + 1))
                    pool.wait_ge(pool_consts, 14)
                    pool.wait_ge(gcur_done, value)
                    pool.indirect_dma_start(out=xg[k], out_offset=None, in_=xs_rows[:, :],
                                            in_offset=bass.IndirectOffsetOnAxis(ap=icur[:, k:k + 1].bitcast(U32), axis=0)).then_inc(xg_loaded[k], 16)

                def scatter(e, k):
                    value = in_register(at(y_done, l, e + 2))
                    pool.wait_ge(pool_consts, 14)
                    pool.wait_ge(y_done, value)
                    pool.tensor_copy(icur[:, 2 + k:3 + k], table[:, bass.ds(e * G4, 1)]).then_inc(dcur_done, 1)
                    value = in_register(at(dcur_done, l, e + 1))
                    pool.wait_ge(pool_consts, 14)
                    pool.wait_ge(dcur_done, value)
                    pool.indirect_dma_start(out=y_rows[:, :], out_offset=bass.IndirectOffsetOnAxis(
                        ap=icur[:, 2 + k:3 + k].bitcast(U32), axis=0), in_=ysb[k], in_offset=None,
                        bounds_check=TOPK * SEQ - 1, oob_is_err=False).then_inc(y_stored[k], 16)

                def overflow(e):
                    def body(b, n):
                        pool.tensor_copy(icur[:, 4:5], gidx[:, bass.ds(e * G4 + b, 1)]).then_inc(o_icur, 1)
                        pool.tensor_copy(icur[:, 5:6], table[:, bass.ds(e * G4 + b, 1)]).then_inc(o_icur, 1)
                        value = in_register(2 * n)
                        pool.wait_ge(pool_consts, 14)
                        pool.wait_ge(o_icur, value)
                        pool.indirect_dma_start(out=o_xg, out_offset=None, in_=xs_rows[:, :],
                                                in_offset=bass.IndirectOffsetOnAxis(ap=icur[:, 4:5].bitcast(U32), axis=0)).then_inc(o_gath, 16)
                        value = n
                        pool.wait_ge(pool_consts, 14)
                        pool.wait_ge(o_y, value)
                        pool.indirect_dma_start(out=y_rows[:, :], out_offset=bass.IndirectOffsetOnAxis(
                            ap=icur[:, 5:6].bitcast(U32), axis=0), in_=o_ysb, in_offset=None,
                            bounds_check=TOPK * SEQ - 1, oob_is_err=False).then_inc(o_st, 16)
                        value = in_register(16 * n)
                        pool.wait_ge(pool_consts, 14)
                        pool.wait_ge(o_st, value)
                    overflow_blocks(pool, e, done, body)

                def gather_next(e, k):
                    value = in_register(at(t1_ready, l, e + 1))
                    pool.wait_ge(pool_consts, 14)
                    pool.wait_ge(t1_ready, value)
                    gather(e + 2, k)

                gather(0, 0)
                gather(1, 1)
                gather_next(0, 0)
                overflow(0)
                gather_next(1, 1)

                def step(s, k, more=True):
                    overflow(s)
                    scatter(s - 1, 1 - k)
                    if more:
                        gather_next(s + 1, 1 - k)

                with pool.Fori(0, E // 2 - 2) as j:
                    step(2 * j + 1, 1)
                    step(2 * j + 2, 0)
                for e in range(E - 3, E):
                    step(e, e % 2, more=False)
                scatter(E - 1, 1)
                values = [in_register(at(y_stored[i], l, 8 * E)) for i in range(2)]
                pool.wait_ge(pool_consts, 14)
                for i in range(2):
                    pool.wait_ge(y_stored[i], values[i])
                for t in range(NT):
                    if t >= 2:
                        value = in_register(at(x2_done, l, t - 1))
                        pool.wait_ge(pool_consts, 14)
                        pool.wait_ge(x2_done, value)
                    pool.dma_start(yc[t % 2], y_rows[2 * P * t:2 * P * (t + 1), :].rearrange("(p k) d -> p k d", k=TOPK)).then_inc(yc_loaded[t % 2], 16)
                value = in_register(at(x2_done, l, NT))
                pool.wait_ge(pool_consts, 14)
                pool.wait_ge(x2_done, value)

        @block.scalar
        def _(act):
            done = act.alloc_register("act_ovf")
            act.reg_mov(done, 0)
            act.wait_ge(cond_t, 1)
            act.activation(a1[:, :], PS[:, 2, 0:C], ACT.Sigmoid).then_inc(cond_sig, 1)
            act.wait_ge(trig, 1)
            act.activation(sinr[:, :, :], sinr[:, :, :], ACT.Sin)
            act.activation(cosr[:, :, :], cosr[:, :, :], ACT.Sin).then_inc(trig_act, 1)
            act.wait_ge(x_loaded, 16)
            act.wait_ge(dve_consts, 1)
            eps, one = cst[:, 0:1], cst[:, 1:2]

            with act.Fori(0, DEPTH) as l:
                def norm_tokens(r):
                    for t in range(NT):
                        if r == 1:
                            act.wait_ge(x_done, at(x_done, l, NT + t + 1))
                        act.activation(hT[:, 2 * t:2 * t + 2, :], xt[:, t, :].rearrange("p (a s) -> p a s", a=2), ACT.Square,
                                       accum_out=ss[:, t:t + 1])
                    act.drain()
                    act.activation(ss[:, :], ss[:, :], ACT.Sqrt, scale=1.0 / D, bias=eps).then_inc(root, 1)

                def copy_hT(r, scale, shift):
                    for k in range(C):
                        act.wait_ge(ht_ready, at(ht_ready, l, C * r + k + 1))
                        act.activation(hT[:, k, :], PS[:, k, :], ACT.Identity, scale=scale[:, k:k + 1],
                                       bias=shift[:, k:k + 1]).then_inc(ht_done, 1)

                def copy_grow(r):
                    act.wait_ge(grow_ready, at(grow_ready, l, r + 1))
                    act.activation(grow[:, :].rearrange("p (a s) -> p a s", a=2), PS[:, 3:5, :], ACT.Copy).then_inc(grow_done, 1)

                norm_tokens(0)
                act.wait_ge(diag_done, at(diag_done, l, 1))
                copy_grow(0)
                copy_hT(0, a1, pc[:, R_SH1:R_SH1 + C])
                act.wait_ge(a_ready, at(a_ready, l, 1))
                act.activation(aT, PS[0:GLA_RANK, 0, :], ACT.Copy).then_inc(a_done, 1)
                for t in range(NT):
                    act.wait_ge(v_ready, at(v_ready, l, t + 1))
                    act.activation(v[:, t, :], PS[:, 4 + t, :], ACT.Copy).then_inc(v_done, 1)
                for m in range(2):
                    act.wait_ge(u_ready, at(u_ready, l, m + 1))
                    act.activation(la[:, m, :], PS[:, m, :], ACT.Identity, bias=pc[:, R_BA + m:R_BA + m + 1]).then_inc(u_done, 1)
                act.drain()
                act.activation(bb, la, ACT.Abs).then_inc(labs, 1)
                act.drain()
                act.activation(bb, bb, ACT.Exp, scale=-1.0)
                act.drain()
                act.activation(bb, bb, ACT.Ln, bias=one).then_inc(lln, 1)
                act.wait_ge(b_done, at(b_done, l, 1))
                act.activation(qdec, bb, ACT.Exp, scale=1.0 / GLA_TAU)
                act.activation(decay[:, :, :], bb.rearrange("p m (n s) -> p m n s", s=CHUNK)[:, :, :, CHUNK - 1], ACT.Exp,
                               scale=1.0 / GLA_TAU)
                act.activation(kinv, bb, ACT.Exp, scale=-1.0 / GLA_TAU).then_inc(eplus, 1)
                act.wait_ge(dif_done, at(dif_done, l, 1))
                act.activation(kend, la, ACT.Exp, scale=-1.0 / GLA_TAU).then_inc(eend, 1)
                for m in range(GH):
                    act.wait_ge(r_ready, at(r_ready, l, m + 1))
                    act.activation(rs[:, m, :], PS[:, (6 + m) % 8, :], ACT.Sigmoid).then_inc(r_sig, 1)
                for t in range(NT):
                    act.wait_ge(sq_ready, at(sq_ready, l, t + 1))
                    act.activation(qk[:, t, 0:QH, :], PS[:, 2 + t, :].rearrange("p (h d) -> p h d", d=HD), ACT.Copy).then_inc(sq_done, 1)
                for t in range(NT):
                    act.wait_ge(skv_ready, at(skv_ready, l, t + 1))
                    b = (6 + t) % 8
                    act.activation(qk[:, t, QH:NN, :], PS[:, b, 0:KVH * HD].rearrange("p (h d) -> p h d", d=HD), ACT.Copy)
                    act.activation(v_tm[:, t, :], PS[:, b, KVH * HD:2 * KVH * HD], ACT.Copy).then_inc(skv_done, 1)
                for h in range(GH):
                    act.wait_ge(o_ready, at(o_ready, l, h + 1))
                    act.activation(osq, PS[:, 4 + h, :], ACT.Square).then_inc(osq_done, 1)
                    act.wait_ge(ms_ready, at(ms_ready, l, h + 1))
                    if h >= 1:
                        act.wait_ge(o_done, at(o_done, l, h))
                    act.activation(orr, PS[:, h, :], ACT.Sqrt, scale=1.0 / P, bias=eps).then_inc(orr_done, 1)
                for i in range(2):
                    if i == 0:
                        act.wait_ge(s_done, at(s_done, l, 1))
                    else:
                        act.wait_ge(qss_done, at(qss_done, l, 1))
                    act.activation(sqt, qk[:, 2 * i:2 * i + 2, :, :].rearrange("p t h d -> p (t h d)"), ACT.Square).then_inc(qsq_done, 1)
                act.wait_ge(qss_done, at(qss_done, l, 2))
                act.activation(qss[:, :, :], qss[:, :, :], ACT.Sqrt, scale=1.0 / HD, bias=eps).then_inc(qrt_done, 1)
                for t in range(NT):
                    act.wait_ge(qT_ready, at(qT_ready, l, t + 1))
                    act.activation(qT[:, :, t * P:t * P + P], PS[:, t, :].rearrange("p (a s) -> p a s", s=P), ACT.Copy).then_inc(qT_done, 1)
                for n in range(NT):
                    lo = P if n == 0 else 0
                    act.wait_ge(max_done, at(max_done, l, n + 1))
                    act.activation(snk[:, n % 2, :], snk[:, n % 2, :], ACT.Exp)
                    for j in range(QH):
                        a = act.activation(sc[n % 2][:, j, lo:], sc[n % 2][:, j, lo:], ACT.Exp, bias=nmax[:, n % 2, j:j + 1],
                                           accum_out=ssum[:, n % 2, j:j + 1])
                    a.then_inc(p_exp, 1)
                    for b in range(1 if n == 0 else 0, 2):
                        i = 2 * n + b - 1
                        act.wait_ge(pTa_ready, at(pTa_ready, l, i + 1))
                        act.activation(pT[:, b, 0:4, :], PS[:, 4 + b, :].rearrange("p (j s) -> p j s", s=P), ACT.Copy).then_inc(pTa_done, 1)
                    act.wait_ge(pv_ready, at(pv_ready, l, n + 1))
                    act.activation(oTs[:, :, n * P:n * P + P], PS[:, 7, :].rearrange("p (a s) -> p a s", s=P), ACT.Copy).then_inc(pv_done, 1)
                for j in range(C):
                    if j >= 2:
                        act.wait_ge(mx_done, at(mx_done, l, j - 1))
                    for i in range(2):
                        act.wait_ge(mx_ready, at(mx_ready, l, 4 * j + i + 1))
                        act.activation(sig[j % 2][:, i, :], PS[:, 4 * (j % 2) + i, :], ACT.Sigmoid).then_inc(mx_sig, 1)
                norm_tokens(1)
                copy_hT(1, a2, pc[:, R_SH2:R_SH2 + C])
                act.wait_ge(lg_ready, at(lg_ready, l, 1))
                act.activation(rt[:, 0, :], PS[:, 0, 0:NT * E], ACT.Sigmoid).then_inc(aff_done, 1)
                copy_grow(1)

                def affine(dst):
                    for k in range(C):
                        a = act.activation(dst[:, k, :], PS[:, 2 + k // 4, P * (k % 4):P * (k % 4) + P], ACT.Identity,
                                           scale=a2[:, k:k + 1], bias=pc[:, R_SH2 + k:R_SH2 + k + 1])
                    return a

                def tokens(e, k):
                    act.wait_ge(t1_ready, at(t1_ready, l, e + 1))
                    affine(xgT[k]).then_inc(t1_done, 1)

                def gate(e, k):
                    act.wait_ge(g_ready, at(g_ready, l, e + 1))
                    act.activation(msig[k], PS[:, 0, :], ACT.Sigmoid).then_inc(sig_done, 1)

                def hidden(e, k):
                    act.wait_ge(t2_ready, at(t2_ready, l, e + 1))
                    act.activation(maT[k], PS[:, 4, :].rearrange("p (f s) -> p f s", s=P), ACT.Copy).then_inc(t2_done, 1)

                def overflow(e):
                    def body(b, n):
                        act.wait_ge(o_t1, n)
                        affine(o_xgT).then_inc(o_t1c, 1)
                        act.wait_ge(o_gu, n)
                        act.activation(o_sig, PS[:, 0, :], ACT.Sigmoid).then_inc(o_sg, 1)
                        act.wait_ge(o_t2, n)
                        act.activation(o_aT, PS[:, 4, :].rearrange("p (f s) -> p f s", s=P), ACT.Copy).then_inc(o_t2c, 1)
                    overflow_blocks(act, e, done, body)

                act.wait_ge(row_done, at(row_done, l, 1))
                tokens(0, 0)
                gate(0, 0)
                overflow(0)
                tokens(1, 1)

                def step(s, k, more=True):
                    gate(s, k)
                    overflow(s)
                    hidden(s - 1, 1 - k)
                    if more:
                        tokens(s + 1, 1 - k)

                with act.Fori(0, E // 2 - 1) as j:
                    step(2 * j + 1, 1)
                    step(2 * j + 2, 0)
                step(E - 1, 1, more=False)
                hidden(E - 1, 1)
                act.wait_ge(x2_done, at(x2_done, l, NT))

        @block.tensor
        def _(pe):
            done = pe.alloc_register("pe_ovf")
            pe.reg_mov(done, 0)
            pe.wait_ge(pool_consts, 11)
            pe.wait_ge(const_loaded, 16 * 9)
            pe.transpose(PS[:, 2, 0:C], crow, ident[0:C, 0:C]).then_inc(cond_t, 1)
            for i in range(DEPTH):
                mm = pe.transpose(PS[:, 3, i * R_END:i * R_END + R_END], params[:, i, :], ident[0:R_END, 0:R_END])
            mm.then_inc(pcs_ready, 1)
            pe.wait_ge(cond_done, 1)

            with pe.Fori(0, DEPTH) as l:
                def wait_unit(u):
                    pe.wait_ge(loaded[u % SLOTS], at(loaded[u % SLOTS], l, 16 * (u // SLOTS + 1)))

                for u in range(ADA):
                    pe.wait_ge(ada_ready, at(ada_ready, l, u + 1))
                    for i in range(4):
                        mm = pe.matmul(PS[:, 7, 4 * u + i:4 * u + i + 1], ada_acc[u % 2][:, i * P:i * P + P], ones[:, 0:1],
                                       start=True, stop=True)
                    mm.then_inc(ada_summed, 1)

                def gate_rows(r):
                    pe.wait_ge(diag_done, at(diag_done, l, r + 1))
                    for h in range(2):
                        mm = pe.matmul(PS[:, 3 + h, :], ones[:, :], diag[:, 4 * h:4 * h + 4, :], start=True, stop=True)
                    mm.then_inc(grow_ready, 1)

                def transpose_tokens(r):
                    pe.wait_ge(xs_ready, at(xs_ready, l, NT * (r + 1)))
                    for k in range(C):
                        for t in range(NT):
                            mm = pe.transpose(PS[:, k, t * P:t * P + P], xs[:, t, k * P:k * P + P], ident[:, :])
                        mm.then_inc(ht_ready, 1)

                gate_rows(0)
                pe.wait_ge(grow_done, at(grow_done, l, 1))
                transpose_tokens(0)

                def channel_major(bank, w, cols):
                    for k in range(C):
                        mm = pe.matmul(PS[0:cols.stop - cols.start, bank, :], w[:, k, cols], hT[:, k, :],
                                       start=(k == 0), stop=(k == C - 1))
                    return mm

                def token_major(bank, t, w, width):
                    for k in range(C):
                        mm = pe.matmul(PS[:, bank, 0:width], hT[:, k, t * P:t * P + P], w[:, k, :],
                                       start=(k == 0), stop=(k == C - 1))
                    return mm

                pe.wait_ge(ht_done, at(ht_done, l, C))
                pe.wait_ge(small_loaded, at(small_loaded, l, 16))
                channel_major(0, w_a, slice(0, GLA_RANK)).then_inc(a_ready, 1)
                wait_unit(U_V)
                for t in range(NT):
                    token_major(4 + t, t, slot(U_V), GV).then_inc(v_ready, 1)
                pe.wait_ge(a_done, at(a_done, l, 1))
                pe.wait_ge(par_loaded, at(par_loaded, l, 16 * 4))
                for m in range(2):
                    pe.matmul(PS[:, m, :], walpha[:, m * P:m * P + P], aT, start=True, stop=True).then_inc(u_ready, 1)
                wait_unit(U_QK)
                for m in range(4):
                    if m == 2:
                        pe.wait_ge(v_done, at(v_done, l, 2))
                    channel_major(2 + m, slot(U_QK), slice(m * P, m * P + P)).then_inc(qk_ready, 1)
                wait_unit(U_R)
                for m in range(GH):
                    if m == 0:
                        pe.wait_ge(v_done, at(v_done, l, NT))
                    if m == 2:
                        pe.wait_ge(u_done, at(u_done, l, 2))
                    channel_major((6 + m) % 8, slot(U_R), slice(m * P, m * P + P)).then_inc(r_ready, 1)
                wait_unit(U_SQ)
                for t in range(NT):
                    pe.wait_ge(qk_done, at(qk_done, l, 1 if t < 2 else 3))
                    token_major(2 + t, t, slot(U_SQ), QH * HD).then_inc(sq_ready, 1)
                pe.wait_ge(small_loaded, at(small_loaded, l, 32))
                for t in range(NT):
                    pe.wait_ge(r_done, at(r_done, l, t + 1))
                    token_major((6 + t) % 8, t, w_kv, 2 * KVH * HD).then_inc(skv_ready, 1)

                pe.wait_ge(sq_done, at(sq_done, l, NT))
                for i in range(2):
                    for t in range(2 * i, 2 * i + 2):
                        for m in range(2):
                            o = ((t % 2) * 2 + m) * P
                            mm = pe.transpose(PS[:, 2 + i, o:o + P], kend[:, m, t * P:t * P + P], ident[:, :])
                    mm.then_inc(kt_ready, 1)
                pe.wait_ge(const_loaded, 16 * 9)
                pe.wait_ge(kt_done, at(kt_done, l, 2))
                pe.wait_ge(skv_done, at(skv_done, l, NT))
                for m in range(2):
                    for r in range(2):
                        for n in range(r, NCH - 1, 2):
                            for h in range(2):
                                rows = slice(CHUNK * r, CHUNK * r + CHUNK)
                                mm = pe.matmul(PS[HD * h:HD * h + HD, 4 + 2 * m + r, (n // 2) * P:(n // 2) * P + P],
                                               kend_tm[rows, n // 2, m * P + HD * h:m * P + HD * h + HD],
                                               v[rows, n // 2, (2 * m + h) * P:(2 * m + h) * P + P], start=True, stop=True,
                                               skip_group_check=True)
                        mm.then_inc(kv_ready, 1)
                for h in range(GH):
                    rows = slice(HD * (h % 2), HD * (h % 2) + HD)
                    for t in range(NT):
                        mm = pe.matmul(PS[:, h, t * P:t * P + P], kinv[rows, h // 2, t * P:t * P + P],
                                       qdec[rows, h // 2, t * P:t * P + P], start=True, stop=True)
                    mm.then_inc(att_ready, 1)
                for h in range(GH):
                    rows = slice(HD * (h % 2), HD * (h % 2) + HD)
                    pe.wait_ge(att_done, at(att_done, l, h + 1))
                    pe.wait_ge(s_done, at(s_done, l, 1))
                    for t in range(NT):
                        pe.matmul(PS[:, 4 + h, t * P:t * P + P], v[:, t, h * P:h * P + P], attm[:, h % 2, t, :],
                                  start=(t == 0), stop=False, skip_group_check=True)
                    for n in range(1, NCH):
                        mm = pe.matmul(PS[:, 4 + h, n * CHUNK:n * CHUNK + CHUNK], S[rows, h // 2, n, :],
                                       qdec[rows, h // 2, n * CHUNK:n * CHUNK + CHUNK], start=False, stop=(n == NCH - 1),
                                       skip_group_check=True)
                    mm.then_inc(o_ready, 1)
                for h in range(GH):
                    pe.wait_ge(osq_done, at(osq_done, l, h + 1))
                    pe.matmul(PS[:, h, :], ones[:, :], osq, start=True, stop=True).then_inc(ms_ready, 1)

                pe.wait_ge(orr_done, at(orr_done, l, GH))
                pe.wait_ge(rope_done, at(rope_done, l, 1))
                for t in range(NT):
                    for a in range(QH // 2):
                        mm = pe.transpose(PS[:, t, a * P:a * P + P], qk[:, t, 2 * a:2 * a + 2, :].rearrange("p h d -> p (h d)"), ident[:, :])
                    mm.then_inc(qT_ready, 1)
                    for g in range(KVH):
                        mm = pe.transpose(PS[:, 4 + t, g * P:g * P + P], kd[:, t, g, :, :].rearrange("p r d -> p (r d)"), ident[:, :])
                    mm.then_inc(kT_ready, 1)
                pe.wait_ge(qT_done, at(qT_done, l, NT))
                pe.wait_ge(kT_done, at(kT_done, l, NT))

                def scores(n):
                    if n >= 1:
                        pe.wait_ge(sc_read, at(sc_read, l, n))
                    lo = P if n == 0 else 0
                    for j in range(QH):
                        g, s, a = j // 4, (j % 4) // 2, j % 2
                        rows = slice(HD * s, HD * s + HD)
                        mm = pe.matmul(PS[:, j // 2, 2 * P * a + lo:2 * P * a + 2 * P], qT[rows, 2 * g + a, n * P:n * P + P],
                                       kT[rows, g, (n - 1) * P + lo:(n + 1) * P], start=True, stop=True)
                    mm.then_inc(sc_ready, 1)

                scores(0)
                for n in range(NT):
                    if n + 1 < NT:
                        scores(n + 1)
                    pe.wait_ge(p_done, at(p_done, l, n + 1))
                    first = 1 if n == 0 else 0
                    for b in range(first, 2):
                        i = 2 * n + b - 1
                        for j in range(4):
                            mm = pe.transpose(PS[:, 4 + b, j * P:j * P + P], sc[n % 2][:, j, b * P:b * P + P], ident[:, :])
                        mm.then_inc(pTa_ready, 1)
                        if i >= 1:
                            pe.wait_ge(pTd_done, at(pTd_done, l, i))
                        for j in range(4):
                            mm = pe.transpose(PS[:, 6, j * P:j * P + P], sc[n % 2][:, 4 + j, b * P:b * P + P], ident[:, :])
                        mm.then_inc(pTd_ready, 1)
                    pe.wait_ge(pTa_done, at(pTa_done, l, 2 * n + 1))
                    pe.wait_ge(pTd_done, at(pTd_done, l, 2 * n + 1))
                    if n >= 1:
                        pe.wait_ge(pv_done, at(pv_done, l, n))
                    for j in range(QH):
                        g, s, a = j // 4, (j % 4) // 2, j % 2
                        for b in range(first, 2):
                            mm = pe.matmul(PS[HD * s:HD * s + HD, 7, (2 * g + a) * P:(2 * g + a) * P + P],
                                           v_tm[:, n - 1 + b, g * HD:g * HD + HD], pT[:, b, j, :],
                                           start=(g == 0 and a == 0 and b == first), stop=(b == 1), skip_group_check=True)
                    mm.then_inc(pv_ready, 1)

                for j in range(C):
                    b0 = 4 * (j % 2)
                    half, cols = j // 4, slice((j % 4) * P, (j % 4) * P + P)
                    if j == 1:
                        pe.wait_ge(pv_done, at(pv_done, l, NT))
                    if j >= 2:
                        pe.wait_ge(mx_done, at(mx_done, l, j - 1))
                    for i, u in enumerate(((U_MA0, U_MB0), (U_MA1, U_MB1))[half]):
                        if j % 4 == 0:
                            wait_unit(u)
                        channel_major(b0 + i, slot(u), cols).then_inc(mx_ready, 1)
                    for i, (u, o) in enumerate(((U_UPG, rs), (U_UPS, oTs))):
                        if j == 0:
                            wait_unit(u)
                            pe.wait_ge(o_done, at(o_done, l, GH))
                            pe.wait_ge(pv_done, at(pv_done, l, NT))
                        for k in range(GH):
                            mm = pe.matmul(PS[:, b0 + 2 + i, :], slot(u, 4)[:, k, j * P:j * P + P], o[:, k, :],
                                           start=(k == 0), stop=(k == GH - 1))
                        mm.then_inc(mx_ready, 1)
                pe.wait_ge(mx_done, at(mx_done, l, C))
                for i in range(2 * NT):
                    t, u = i % NT, U_O0 + i // NT
                    if t == 0:
                        wait_unit(u)
                    for k in range(C):
                        mm = pe.matmul(PS[:, i, :], mT[:, k, t * P:t * P + P], slot(u)[:, k, :], start=(k == 0), stop=(k == C - 1))
                    mm.then_inc(out_ready, 1)

                pe.wait_ge(x_done, at(x_done, l, 2 * NT))
                transpose_tokens(1)
                pe.wait_ge(ht_done, at(ht_done, l, 2 * C))
                for t in range(NT):
                    for k in range(C):
                        mm = pe.matmul(PS[:, 0, t * E:t * E + E], hT[:, k, t * P:t * P + P], wr[:, k, :], start=(k == 0), stop=(k == C - 1))
                mm.then_inc(lg_ready, 1)
                gate_rows(1)
                pe.wait_ge(m_done, at(m_done, l, 1))
                pe.matmul(PS[:, 1, 0:NT * E], before[:, :], rt[:, MASK, :], start=True, stop=True)
                pe.matmul(PS[:, 1, NT * E:2 * NT * E], ones[:, :], rt[:, MASK, :], start=True, stop=True).then_inc(rk_ready, 1)
                pe.wait_ge(row_done, at(row_done, l, 1))
                pe.wait_ge(grow_done, at(grow_done, l, 2))

                def tokens(src, raise_at_first=None):
                    for k in range(C):
                        mm = pe.transpose(PS[:, 2 + k // 4, (k % 4) * P:(k % 4) * P + P], src[:, k * P:k * P + P], ident[:, :])
                        if k == 0 and raise_at_first is not None:
                            mm.then_inc(raise_at_first, 1)
                    return mm

                def up_product(bank, xT, w):
                    for k in range(C):
                        mm = pe.matmul(PS[:, bank, :], xT[:, k, :], w[:, k, :], start=(k == 0), stop=(k == C - 1))
                    return mm

                def hidden(src, raise_at_first=None):
                    for f in range(FC):
                        mm = pe.transpose(PS[:, 4, f * P:f * P + P], src[:, f * P:f * P + P], ident[:, :])
                        if f == 0 and raise_at_first is not None:
                            mm.then_inc(raise_at_first, 1)
                    return mm

                def down_product(aT_, w):
                    for h in range(2):
                        for f in range(FC):
                            mm = pe.matmul(PS[:, 5 + h, :], aT_[:, f, :], w[:, f, 512 * h:512 * h + 512], start=(f == 0), stop=(f == FC - 1))
                    return mm

                def weights(k, part):
                    return slot(U_MOE + 3 * k + part, (C, C, FC)[part])

                def wait_weights(pair, k, part):
                    s = loaded[3 * k + part]
                    pe.wait_ge(s, at(s, l, 16 * (U_MOE // SLOTS + 1) + 16 * pair))

                def gate_up(e, pair, k):
                    pe.wait_ge(t1_done, at(t1_done, l, e + 1))
                    wait_weights(pair, k, 0)
                    up_product(0, xgT[k], weights(k, 0)).then_inc(g_ready, 1)
                    wait_weights(pair, k, 1)
                    up_product(1, xgT[k], weights(k, 1)).then_inc(u2_ready, 1)

                def transposed_tokens(e, pair, k, raise_at_first=None):
                    pe.wait_ge(xg_loaded[k], at(xg_loaded[k], l, 16 * pair + 16))
                    tokens(xg[k], raise_at_first).then_inc(t1_ready, 1)

                def finish_a(e, k):
                    pe.wait_ge(act_done, at(act_done, l, e + 1))
                    hidden(mact[k], gu_free).then_inc(t2_ready, 1)

                def finish_b(e, pair, k):
                    pe.wait_ge(t2_done, at(t2_done, l, e + 1))
                    wait_weights(pair, k, 2)
                    pe.wait_ge(y_done, at(y_done, l, e + 1))
                    down_product(maT[k], weights(k, 2)).then_inc(d_ready, 1)

                def overflow(e, pair, k, y_before):
                    def body(b, n):
                        pe.wait_ge(o_gath, 16 * n)
                        tokens(o_xg).then_inc(o_t1, 1)
                        pe.wait_ge(act_done, at(act_done, l, e + 1))
                        pe.wait_ge(o_t1c, n)
                        up_product(0, o_xgT, weights(k, 0))
                        up_product(1, o_xgT, weights(k, 1)).then_inc(o_gu, 1)
                        pe.wait_ge(o_ac, n)
                        hidden(o_act).then_inc(o_t2, 1)
                        pe.wait_ge(o_t2c, n)
                        wait_weights(pair, k, 2)
                        pe.wait_ge(y_done, at(y_done, l, y_before))
                        down_product(o_aT, weights(k, 2)).then_inc(o_d, 1)
                        pe.wait_ge(o_y, n)
                    overflow_blocks(pe, e, done, body)

                transposed_tokens(0, 0, 0)
                gate_up(0, 0, 0)
                overflow(0, 0, 0, 1)
                transposed_tokens(1, 0, 1, gu_free)

                def step(s, pair, k, pair_before, more=True):
                    pe.wait_ge(act_done, at(act_done, l, s))
                    gate_up(s, pair, k)
                    overflow(s, pair, k, s)
                    finish_a(s - 1, 1 - k)
                    if more:
                        transposed_tokens(s + 1, pair + k, 1 - k)
                    finish_b(s - 1, pair_before, 1 - k)

                with pe.Fori(0, E // 2 - 1) as j:
                    step(2 * j + 1, j, 1, j)
                    step(2 * j + 2, j + 1, 0, j)
                step(E - 1, E // 2 - 1, 1, E // 2 - 1, more=False)
                pe.wait_ge(act_done, at(act_done, l, E))
                hidden(mact[1]).then_inc(t2_ready, 1)
                finish_b(E - 1, E // 2 - 1, 1)

        @block.vector
        def _(dve):
            tt, ts, stt = dve.tensor_tensor, dve.tensor_scalar, dve.scalar_tensor_tensor
            done = dve.alloc_register("dve_ovf")
            dve.reg_mov(done, 0)
            dve.memset(cst[:, 0:1], EPS)
            dve.memset(cst[:, 1:2], 1.0)
            dve.memset(cst[:, 2:3], 0.0).then_inc(dve_consts, 1)
            dve.wait_ge(const_loaded, 16 * 9)
            pf = rt[:, 0, 0:NT]
            ang = rt[:, 1, 0:NT * HALF].rearrange("p (t i) -> p t i", t=NT)
            turn = rt[:, 2, 0:NT * HALF].rearrange("p (t i) -> p t i", t=NT)
            dve.tensor_copy(pf, posi[:, :])
            dve.drain()
            freq = np.power(np.float32(ROPE_THETA), -np.arange(HALF, dtype=np.float32) / np.float32(HALF))
            for i in range(HALF):
                ts(ang[:, :, i:i + 1], pf.unsqueeze(2), float(freq[i]), None, ALU.mult)
            dve.drain()
            round_to = 1.5 * 2.0 ** 23
            ts(turn, ang, float(1 / (2 * np.pi)), round_to, ALU.mult, ALU.add)
            dve.drain()
            ts(turn, turn, -round_to, None, ALU.add)
            dve.drain()
            two_pi_hi = 6.28125
            mid = np.float32(2 * np.pi - two_pi_hi)
            mid = float((mid.view(np.uint32) & np.uint32(0xFFFFF000)).view(np.float32))
            for part in (two_pi_hi, mid, float(2 * np.pi - two_pi_hi - mid)):
                stt(ang, turn, -part, ang, ALU.mult, ALU.add)
                dve.drain()
            ts(sinr[:, :, :], ang, -3.1415925, 3.1415925, ALU.max, ALU.min)
            dve.drain()
            ts(turn, sinr[:, :, :], -1.0, None, ALU.mult)
            dve.drain()
            tt(turn, turn, sinr[:, :, :], ALU.max)
            dve.drain()
            ts(cosr[:, :, :], turn, -1.0, float(np.pi / 2), ALU.mult, ALU.add).then_inc(trig, 1)
            dve.wait_ge(cond_sig, 1)
            tt(condT[:, :], PS[:, 2, 0:C], a1[:, :], ALU.mult).then_inc(cond_done, 1)
            dve.wait_ge(pcs_ready, 1)
            dve.tensor_copy(pcs[:, :, :].rearrange("p l n -> p (l n)"), PS[:, 3, 0:DEPTH * R_END])
            dve.wait_ge(pool_consts, 14)
            dve.wait_ge(x_loaded, 16)
            dve.wait_ge(trig_act, 1)

            with dve.Fori(0, DEPTH) as l:
                def norm_tokens(r):
                    dve.wait_ge(root, at(root, l, r + 1))
                    dve.reciprocal(rstd[:, :], ss[:, :])
                    dve.drain()
                    for t in range(NT):
                        ts(xs[:, t, :], xt[:, t, :], rstd[:, t:t + 1], None, ALU.mult).then_inc(xs_ready, 1)

                def gate_diagonal(row):
                    tt(diag, ident[:, :].unsqueeze(1).broadcast_to([P, C, P]),
                       pc[:, row:row + C].unsqueeze(2).broadcast_to([P, C, P]), ALU.mult).then_inc(diag_done, 1)

                norm_tokens(0)
                for u in range(ADA):
                    dve.wait_ge(loaded[u % SLOTS], at(loaded[u % SLOTS], l, 16 * (u // SLOTS + 1)))
                    if u >= 2:
                        dve.wait_ge(ada_summed, at(ada_summed, l, u - 1))
                    acc = ada_acc[u % 2]
                    product = ts(acc, slot(u)[:, 0, :], condT[:, 0:1], None, ALU.mult)
                    for k in range(1, C):
                        dve.drain()
                        product = stt(acc, slot(u)[:, k, :], condT[:, k:k + 1], acc, ALU.mult, ALU.add)
                    product.then_inc(ada_ready, 1)
                dve.wait_ge(ada_summed, at(ada_summed, l, ADA))
                tt(pc[:, 0:R_NM], PS[:, 7, 0:R_NM], pcs[:, bass.ds(l, 1), 0:R_NM].rearrange("p a n -> p (a n)"), ALU.add)
                ts(pc[:, R_NM:], pcs[:, bass.ds(l, 1), R_NM:].rearrange("p a n -> p (a n)"), 1.0, None, ALU.mult)
                dve.drain()
                stt(a1[:, :], pc[:, R_SC1:R_SC1 + C], 1.0, pc[:, R_NM:R_NM + C], ALU.add, ALU.mult)
                stt(a2[:, :], pc[:, R_SC2:R_SC2 + C], 1.0, pc[:, R_NF:R_NF + C], ALU.add, ALU.mult)
                gate_diagonal(R_G1)

                dve.wait_ge(labs, at(labs, l, 1))
                ts(la, la, 0.0, None, ALU.min)
                dve.drain()
                dve.wait_ge(lln, at(lln, l, 1))
                tt(la, la, bb, ALU.subtract)
                dve.drain()
                dve.wait_ge(scanm_made, at(scanm_made, l, 2))
                for m in range(2):
                    scan = dve.tensor_tensor_scan(bb[:, m, :], scanm, la[:, m, :], 0.0, ALU.mult, ALU.add)
                scan.then_inc(b_done, 1)
                dve.drain()
                per_chunk = bb.rearrange("p m (n s) -> p (m n) s", s=CHUNK)
                tt(la.rearrange("p m (n s) -> p (m n) s", s=CHUNK), per_chunk,
                   per_chunk[:, :, CHUNK - 1:CHUNK].broadcast_to([P, 2 * NCH, CHUNK]), ALU.subtract).then_inc(dif_done, 1)
                dve.wait_ge(eplus, at(eplus, l, 1))
                dve.wait_ge(qk_ready, at(qk_ready, l, 2))
                stt(qdec, PS[:, 2:4, :], float(HD) ** -0.5, qdec, ALU.mult, ALU.mult).then_inc(qk_done, 1)
                dve.wait_ge(qk_ready, at(qk_ready, l, 4))
                tt(kinv, PS[:, 4:6, :], kinv, ALU.mult).then_inc(qk_done, 1)
                dve.wait_ge(eend, at(eend, l, 1))
                tt(kend, PS[:, 4:6, :], kend, ALU.mult).then_inc(qk_done, 1)
                for h in range(GH):
                    dve.wait_ge(r_sig, at(r_sig, l, h + 1))
                    stt(rs[:, h, :], PS[:, (6 + h) % 8, :], pc[:, R_GN + h:R_GN + h + 1], rs[:, h, :], ALU.mult, ALU.mult).then_inc(r_done, 1)
                for i in range(2):
                    dve.wait_ge(kt_ready, at(kt_ready, l, i + 1))
                    dve.tensor_copy(kend_tm[:, 2 * i:2 * i + 2, :], PS[:, 2 + i, :].rearrange("p (t n) -> p t n", t=2)).then_inc(kt_done, 1)

                dve.wait_ge(skv_ready, at(skv_ready, l, NT))
                dve.memset(attm[:, :, :, :], 0.0)
                dve.drain()

                def mask_scores(h):
                    dve.wait_ge(x_loaded, 16)
                    dve.wait_ge(att_ready, at(att_ready, l, h + 1))
                    if h >= 2:
                        dve.wait_ge(o_ready, at(o_ready, l, h - 1))
                    dve.copy_predicated(attm[:, h % 2, :, :], causal[:, :].bitcast(U32).unsqueeze(1).broadcast_to([P, NT, P]),
                                        PS[:, h, :].rearrange("p (t s) -> p t s", t=NT)).then_inc(att_done, 1)

                dve.wait_ge(kv_ready, at(kv_ready, l, 4))
                for m in range(2):
                    dve.tensor_copy(S[:, m, 1, :], PS[:, 4 + 2 * m, 0:P])
                for n in range(1, NCH - 1):
                    dve.drain()
                    for m in range(2):
                        step = stt(S[:, m, n + 1, :], S[:, m, n, :], decay[:, m, n:n + 1],
                                   PS[:, 4 + 2 * m + n % 2, (n // 2) * P:(n // 2) * P + P], ALU.mult, ALU.add)
                step.then_inc(s_done, 1)
                for h in range(GH):
                    mask_scores(h)
                for h in range(GH):
                    dve.wait_ge(orr_done, at(orr_done, l, h + 1))
                    dve.reciprocal(orr, orr)
                    dve.drain()
                    tt(orr, PS[:, 4 + h, :], orr, ALU.mult)
                    dve.drain()
                    tt(rs[:, h, :], orr, rs[:, h, :], ALU.mult).then_inc(o_done, 1)

                for i in range(2):
                    dve.wait_ge(qsq_done, at(qsq_done, l, i + 1))
                    dve.tensor_reduce(qss[:, 2 * i:2 * i + 2, :], sqt.rearrange("p (t h d) -> p t h d", t=2, h=NN), AX.X, ALU.add).then_inc(qss_done, 1)
                dve.wait_ge(qrt_done, at(qrt_done, l, 1))
                dve.reciprocal(qss[:, :, :], qss[:, :, :])
                dve.drain()
                heads = qk.rearrange("p t h d -> p (t h) d")
                tt(heads, heads, qss[:, :, :].rearrange("p t h -> p (t h)").unsqueeze(2).broadcast_to([P, NT * NN, HD]), ALU.mult)
                dve.drain()
                for part, hs in enumerate((slice(0, QH), slice(QH, NN))):
                    tt(qk[:, :, hs, :], qk[:, :, hs, :],
                       gains[:, part:part + 1, :].unsqueeze(1).broadcast_to([P, NT, hs.stop - hs.start, HD]), ALU.mult)
                dve.drain()
                x1, x2 = qk[:, :, :, 0:HALF], qk[:, :, :, HALF:2 * HALF]
                w = NT * NN * HALF
                tmp = [sqt[:, w * i:w * i + w].rearrange("p (t h i) -> p t h i", t=NT, h=NN) for i in range(4)]
                cos = cosr[:, :, :].unsqueeze(2).broadcast_to([P, NT, NN, HALF])
                sin = sinr[:, :, :].unsqueeze(2).broadcast_to([P, NT, NN, HALF])
                tt(tmp[0], x1, cos, ALU.mult)
                tt(tmp[1], x2, sin, ALU.mult)
                tt(tmp[2], x2, cos, ALU.mult)
                tt(tmp[3], x1, sin, ALU.mult)
                dve.drain()
                tt(x1, tmp[0], tmp[1], ALU.subtract)
                tt(x2, tmp[2], tmp[3], ALU.add)
                dve.drain()
                for r in range(2):
                    cp = dve.tensor_copy(kd[:, :, :, r, :], qk[:, :, QH:NN, :])
                cp.then_inc(rope_done, 1)
                for t in range(NT):
                    dve.wait_ge(kT_ready, at(kT_ready, l, t + 1))
                    dve.tensor_copy(kT[:, :, t * P:t * P + P], PS[:, 4 + t, 0:2 * P].rearrange("p (g s) -> p g s", g=KVH)).then_inc(kT_done, 1)

                sink_j = sink_t[:, :].rearrange("p (g a s) -> p g s a", g=KVH, s=2)

                def by_head(tile):
                    return tile.rearrange("p (g s a) -> p g s a", g=KVH, s=2)

                def score_max(n):
                    lo = P if n == 0 else 0
                    if n >= 2:
                        dve.wait_ge(pTa_ready, at(pTa_ready, l, 2 * n - 3))
                        dve.wait_ge(pTd_ready, at(pTd_ready, l, 2 * n - 3))
                    dve.wait_ge(sc_ready, at(sc_ready, l, n + 1))
                    stt(sc[n % 2][:, :, lo:], PS[:, 0:4, :].rearrange("p b (a s) -> p (b a) s", a=2)[:, :, lo:], float(HD) ** -0.5,
                        band[:, lo:].unsqueeze(1).broadcast_to([P, QH, 2 * P - lo]), ALU.mult, ALU.add).then_inc(sc_read, 1)
                    dve.drain()
                    dve.tensor_reduce(smax[:, :], sc[n % 2][:, :, lo:], AX.X, ALU.max)
                    dve.drain()
                    tt(by_head(smax[:, :]), by_head(smax[:, :]), sink_j, ALU.max)
                    dve.drain()
                    ts(nmax[:, n % 2, :], smax[:, :], -1.0, None, ALU.mult)
                    tt(by_head(snk[:, n % 2, :]), sink_j, by_head(smax[:, :]), ALU.subtract).then_inc(max_done, 1)

                score_max(0)
                for n in range(NT):
                    lo = P if n == 0 else 0
                    if n + 1 < NT:
                        score_max(n + 1)
                    dve.wait_ge(p_exp, at(p_exp, l, n + 1))
                    tt(ssum[:, n % 2, :], ssum[:, n % 2, :], snk[:, n % 2, :], ALU.add)
                    dve.drain()
                    dve.reciprocal(ssum[:, n % 2, :], ssum[:, n % 2, :])
                    dve.drain()
                    tt(sc[n % 2][:, :, lo:], sc[n % 2][:, :, lo:], ssum[:, n % 2, :].unsqueeze(2).broadcast_to([P, QH, 2 * P - lo]),
                       ALU.mult).then_inc(p_done, 1)
                    for b in range(1 if n == 0 else 0, 2):
                        dve.wait_ge(pTd_ready, at(pTd_ready, l, 2 * n + b))
                        dve.tensor_copy(pT[:, b, 4:8, :], PS[:, 6, :].rearrange("p (j s) -> p j s", s=P)).then_inc(pTd_done, 1)

                for j in range(C):
                    b0 = 4 * (j % 2)
                    for i in range(2):
                        dve.wait_ge(mx_sig, at(mx_sig, l, 2 * j + i + 1))
                        dve.wait_ge(mx_ready, at(mx_ready, l, 4 * j + 3 + i))
                        tt(sig[j % 2][:, i, :], sig[j % 2][:, i, :], PS[:, b0 + 2 + i, :], ALU.mult)
                    dve.drain()
                    tt(mT[:, j, :], sig[j % 2][:, 0, :], sig[j % 2][:, 1, :], ALU.add).then_inc(mx_done, 1)
                dve.wait_ge(grow_done, at(grow_done, l, 1))
                for i in range(2 * NT):
                    t, cols = i % NT, slice(512 * (i // NT), 512 * (i // NT) + 512)
                    dve.wait_ge(out_ready, at(out_ready, l, i + 1))
                    tt(otmp[i % 2], PS[:, i, :], grow[:, cols], ALU.mult)
                    dve.drain()
                    tt(xt[:, t, cols], xt[:, t, cols], otmp[i % 2], ALU.add).then_inc(x_done, 1)
                gate_diagonal(R_G2)
                norm_tokens(1)

                dve.wait_ge(aff_done, at(aff_done, l, 1))
                aff, sel, key = rt[:, 0, :], rt[:, 1, :], rt[:, 2, :]
                tt(sel.rearrange("p (t e) -> p t e", e=E), aff.rearrange("p (t e) -> p t e", e=E),
                   br[:, :].unsqueeze(1).broadcast_to([P, NT, E]), ALU.add)
                dve.drain()
                four = sel.rearrange("p (q a b) -> p q a b", a=2, b=2)
                hi2 = rt[:, 3, 0:2 * NT * G4].rearrange("p (q a) -> p q a", a=2)
                lo2 = rt[:, 4, 0:2 * NT * G4].rearrange("p (q a) -> p q a", a=2)
                tt(hi2, four[:, :, :, 0], four[:, :, :, 1], ALU.max)
                tt(lo2, four[:, :, :, 0], four[:, :, :, 1], ALU.min)
                dve.drain()
                q = NT * G4
                top1, top2, low = rt[:, 5, 0:q], rt[:, 6, 0:q], rt[:, 7, 0:q]
                tt(top1, hi2[:, :, 0], hi2[:, :, 1], ALU.max)
                tt(top2, hi2[:, :, 0], hi2[:, :, 1], ALU.min)
                tt(low, lo2[:, :, 0], lo2[:, :, 1], ALU.max)
                dve.drain()
                tt(top2, top2, low, ALU.max)
                dve.drain()
                tt(top1, top1, top2, ALU.add)
                dve.drain()

                def first_max(score, n, weight, hot, small, keys):
                    rows = score.rearrange("p (t n) -> p t n", n=n)
                    keys, hot = (a.rearrange("p (t n) -> p t n", n=n) for a in (keys, hot))
                    dve.tensor_reduce(small, rows, AX.X, ALU.max)
                    dve.drain()
                    tt(keys, rows, small.unsqueeze(2).broadcast_to([P, NT, n]), ALU.is_equal)
                    dve.drain()
                    tt(keys, keys, weight[:, :].unsqueeze(1).broadcast_to([P, NT, n]), ALU.mult)
                    dve.drain()
                    dve.tensor_reduce(small, keys, AX.X, ALU.max)
                    dve.drain()
                    tt(hot, keys, small.unsqueeze(2).broadcast_to([P, NT, n]), ALU.is_equal)
                    dve.drain()

                small = rt[:, 8, 0:NT]
                group, off = rt[:, 9, 0:q], rt[:, 10, 0:q]
                first_max(top1, G4, wg4, group, small, key[:, 0:q])
                ts(off, group, -1.0, -NEG, ALU.add, ALU.mult)
                tt(sel.rearrange("p (q e) -> p q e", e=G4), sel.rearrange("p (q e) -> p q e", e=G4),
                   group.unsqueeze(2).broadcast_to([P, q, G4]), ALU.mult)
                dve.drain()
                tt(sel.rearrange("p (q e) -> p q e", e=G4), sel.rearrange("p (q e) -> p q e", e=G4),
                   off.unsqueeze(2).broadcast_to([P, q, G4]), ALU.add)
                dve.drain()
                hot = [rt[:, 11, :], rt[:, 12, :]]
                first_max(sel, E, w16, hot[0], small, key)
                stt(sel, hot[0], 3 * NEG, sel, ALU.mult, ALU.add)
                dve.drain()
                first_max(sel, E, w16, hot[1], small, key)
                tt(rt[:, MASK, :], hot[0], hot[1], ALU.add).then_inc(m_done, 1)
                pair = rt[:, 14, 0:2 * NT].rearrange("p (k t) -> p k t", k=TOPK)
                for k in range(TOPK):
                    tt(key, aff, hot[k], ALU.mult)
                    dve.drain()
                    dve.tensor_reduce(pair[:, k, :], key.rearrange("p (t e) -> p t e", e=E), AX.X, ALU.add)
                    dve.drain()
                tt(small, pair[:, 0, :], pair[:, 1, :], ALU.add)
                dve.drain()
                dve.reciprocal(small, small)
                dve.drain()
                tt(wts[:, :, :], pair, small.unsqueeze(1).broadcast_to([P, TOPK, NT]), ALU.mult)
                dve.wait_ge(rk_ready, at(rk_ready, l, 1))
                rank, per_tile = rt[:, 15, :], rt[:, 16, :]
                dve.tensor_copy(rt[:, 15:17, :].rearrange("p a n -> p (a n)"), PS[:, 1, 0:2 * NT * E])
                dve.drain()
                for t in range(1, NT):
                    tt(per_tile[:, t * E:t * E + E], per_tile[:, t * E:t * E + E], per_tile[:, t * E - E:t * E], ALU.add)
                    dve.drain()
                tt(rank[:, E:], rank[:, E:], per_tile[:, 0:(NT - 1) * E], ALU.add)
                dve.tensor_copy(cnt_i[:, :], per_tile[:, (NT - 1) * E:])
                dve.drain()
                blk, row = rt[:, 17, :], rt[:, 18, :]
                ts(blk, rank, float(P), None, ALU.is_ge)
                dve.drain()
                for b in range(2, NT):
                    stt(blk, rank, float(P * b), blk, ALU.is_ge, ALU.add)
                    dve.drain()
                stt(row.rearrange("p (t e) -> p t e", e=E), blk.rearrange("p (t e) -> p t e", e=E), 1.0 - G4 * E * P,
                    e4[:, :].unsqueeze(1).broadcast_to([P, NT, E]), ALU.mult, ALU.add)
                dve.drain()
                stt(row, rank, float(G4 * E), row, ALU.mult, ALU.add)
                dve.drain()
                rows = rt[:, 19, 0:2 * NT].rearrange("p (k t) -> p k t", k=TOPK)
                for k in range(TOPK):
                    tt(key, row, hot[k], ALU.mult)
                    dve.drain()
                    dve.tensor_reduce(rows[:, k, :], key.rearrange("p (t e) -> p t e", e=E), AX.X, ALU.add)
                    dve.drain()
                dve.tensor_copy(row_i[:, :].rearrange("p (k t) -> p k t", k=TOPK), rows).then_inc(row_done, 1)
                dve.wait_ge(tab_loaded, at(tab_loaded, l, 16))
                ts(gidx[:, :], table[:, :], TOPK * SEQ - 1, None, ALU.min)
                dve.drain()
                ts(gidx[:, :], gidx[:, :], 1, None, ALU.arith_shift_right).then_inc(idx_done, 1)
                dve.drain()
                dve.wait_ge(grow_done, at(grow_done, l, 2))
                dve.tensor_copy(rstd[:, :], rstd[:, :]).then_inc(y_done, 1)

                def act_product(dst, s):
                    tt(dst, PS[:, 0, :], s, ALU.mult)
                    dve.drain()
                    return tt(dst, PS[:, 1, :], dst, ALU.mult)

                def outputs(dst):
                    return tt(dst.rearrange("p (a s) -> p a s", a=2), PS[:, 5:7, :], grow[:, :].rearrange("p (a s) -> p a s", a=2), ALU.mult)

                def hidden(e, k):
                    dve.wait_ge(sig_done, at(sig_done, l, e + 1))
                    dve.wait_ge(u2_ready, at(u2_ready, l, e + 1))
                    act_product(mact[k], msig[k]).then_inc(act_done, 1)

                def finish(e, k):
                    dve.wait_ge(d_ready, at(d_ready, l, e + 1))
                    outputs(ysb[k]).then_inc(y_done, 1)

                def overflow(e):
                    def body(b, n):
                        dve.wait_ge(o_sg, n)
                        act_product(o_act, o_sig).then_inc(o_ac, 1)
                        dve.wait_ge(o_d, n)
                        outputs(o_ysb).then_inc(o_y, 1)
                    overflow_blocks(dve, e, done, body)

                hidden(0, 0)
                overflow(0)

                def step(s, k, stored):
                    hidden(s, k)
                    overflow(s)
                    if stored is not None:
                        dve.wait_ge(y_stored[1 - k], at(y_stored[1 - k], l, 16 * stored))
                    finish(s - 1, 1 - k)

                step(1, 1, None)
                step(2, 0, None)
                with dve.Fori(0, E // 2 - 2) as j:
                    step(2 * j + 3, 1, j + 1)
                    step(2 * j + 4, 0, j + 1)
                step(E - 1, 1, E // 2 - 1)
                dve.wait_ge(y_stored[1], at(y_stored[1], l, 16 * (E // 2 - 1)))
                finish(E - 1, 1)
                for t in range(NT):
                    dve.wait_ge(yc_loaded[t % 2], at(yc_loaded[t % 2], l, 16 * (t // 2) + 16))
                    for k in range(TOPK):
                        add = stt(xt[:, t, :], yc[t % 2][:, k, :], wts[:, k, t:t + 1], xt[:, t, :], ALU.mult, ALU.add)
                        if k == 0:
                            dve.drain()
                    add.then_inc(x2_done, 1)


_INS = ['x', 'c', 'positions', 'w_ada', 'b_ada', 'norm_mix', 'w_in', 'w_alpha2', 'b_alpha', 'gla_norm', 'q_norm', 'k_norm',
        'sinks', 'w_up_gla', 'w_up_swa', 'w_out', 'norm_ffn', 'w_router', 'b_router', 'w_gate', 'w_up', 'w_down']


def kernel(**inputs):
    import concourse.bacc as bacc
    from concourse.bass_utils import run_bass_kernel_spmd

    nc = bacc.Bacc("TRN2", target_bir_lowering=False, num_devices=1, dynamic_dma_scratch_size=12288)
    arrays, args = {}, []
    for name in _INS:
        a = np.ascontiguousarray(inputs[name])
        arrays["in_" + name] = a
        args.append(nc.dram_tensor("in_" + name, a.shape, mybir.dt.from_np(a.dtype), kind="ExternalInput").ap())
    x = arrays["in_x"]
    args.append(nc.dram_tensor("out_x", x.shape, mybir.dt.from_np(x.dtype), kind="ExternalOutput").ap())
    trunk(nc, *args)
    return run_bass_kernel_spmd(nc, [arrays], core_ids=[0]).results[0]["out_x"]
```

```python
from contextlib import ExitStack

import numpy as np
import concourse.bass as bass
from concourse import mybir

F32 = mybir.dt.float32
F32R = mybir.dt.float32r
I32 = mybir.dt.int32
U32 = mybir.dt.uint32
ACT = mybir.ActivationFunctionType
ALU = mybir.AluOpType
AX = mybir.AxisListType

P = 128
EPS = 1e-6
NEG = -1e30
GLA_TAU = 16.0
GLA_RANK = 16
CHUNK = 64
ROPE_THETA = 500000.0
SLOTS = 6
MASK = 13


def trunk(nc, x, c, positions, w_ada, b_ada, norm_mix, w_in, w_alpha2, b_alpha, gla_norm,
          q_norm, k_norm, sinks, w_up_gla, w_up_swa, w_out, norm_ffn, w_router, b_router,
          w_gate, w_up, w_down, out):
    _, SEQ, D = x.shape
    DEPTH = w_ada.shape[0]
    NT = SEQ // P
    C = D // P
    E = w_router.shape[1]
    FF = w_gate.shape[3]
    FC = FF // P
    HD = q_norm.shape[1]
    QH = sinks.shape[1]
    KVH = 2
    GW = w_alpha2.shape[2]
    GV = gla_norm.shape[1]
    GH = GW // HD
    NCH = SEQ // CHUNK
    G4 = 4
    HALF = HD // 8
    NN = QH + KVH
    TOPK = 2
    col_qk, col_v = 0, 2 * GW
    col_a = col_v + GV
    col_r = col_a + GLA_RANK
    col_sq = col_r + GV
    col_sk = col_sq + QH * HD
    col_ma = col_sk + 2 * KVH * HD
    col_mb = col_ma + D

    ADA = 6 * D // 512
    ADA_EARLY = 9
    ADA_DVE = 6
    W_SQ, W_KV, W_V, W_QK, W_R, W_MA0, W_MA1, W_UPG, W_MB0, W_MB1, W_UPS, W_O0, W_O1 = range(13)
    UNITS = 13
    assert ADA % SLOTS == 0
    UNIT_SLOTS = (0, 1, 5)
    BEFORE_MOE = [ADA // SLOTS + sum(UNIT_SLOTS[n % 3] == i for n in range(UNITS)) for i in range(SLOTS)]

    R_SH1, R_SC1, R_G1, R_SH2, R_SC2, R_G2, R_NM = (C * i for i in range(7))
    R_NF = R_NM + C
    R_BA = R_NF + C
    R_GN = R_BA + GW // P
    R_END = R_GN + GV // P

    def dram(name, shape, dt=F32):
        return nc.dram_tensor(name, shape, dt, kind="Internal").ap()

    xs_rows = dram("xs_rows", (SEQ, D))
    y_rows = dram("y_rows", (TOPK * SEQ, D))
    slot_table = dram("slot_table", (P * G4 * E, 1), I32)

    with ExitStack() as ctx:
        def sb(name, shape, dt=F32):
            return ctx.enter_context(nc.sbuf_tensor(name, shape, dt))

        def sem(name):
            return ctx.enter_context(nc.semaphore(name))

        shapes = (("ring", [P, SLOTS, 4096]), ("hT", [P, C, SEQ]), ("reg0", [P, 4096]), ("reg23", [P, 4096]),
                  ("reg4", [P, 2048]))
        with ExitStack() as both:
            ring, hT, reg0, reg23, reg4 = [both.enter_context(nc.sbuf_tensor(n, shape, F32)) for n, shape in shapes]
        ring_r, hT_r, reg0_r, reg23_r, reg4_r = [sb(n + "_parts", shape, F32R) for n, shape in shapes]
        xt = sb("xt", [P, NT, D])
        w_a = sb("w_a", [P, C, GLA_RANK])
        grow = sb("grow", [P, D])
        reg1 = sb("reg1", [P, 2048])
        reg5 = sb("reg5", [P, 2048])
        reg6 = sb("reg6", [P, NT * NN * HD])
        reg7 = sb("reg7", [P, 1024])
        v_tm = sb("v_tm", [P, NT, KVH * HD])
        ident = sb("ident", [P, P])
        ones = sb("ones", [P, P])
        before = sb("before", [P, P])
        causal = sb("causal", [P, P])
        band = sb("band", [P, 2 * P])
        cosr = sb("cosr", [P, NT, HALF])
        sinr = sb("sinr", [P, NT, HALF])
        pcs = sb("pcs", [P, DEPTH, R_END])
        pc = sb("pc", [P, R_END])
        a1 = sb("a1", [P, C])
        a2 = sb("a2", [P, C])
        condT = sb("condT", [P, C])
        gains = sb("gains", [P, 2, HD])
        sink_t = sb("sink_t", [P, QH])
        wr = sb("wr", [P, C, E])
        br = sb("br", [P, E])
        ss = sb("ss", [P, NT])
        rstd = sb("rstd", [P, NT])
        qss = sb("qss", [P, NT, NN])
        decay = sb("decay", [P, 2, NCH])
        smax = sb("smax", [P, QH])
        nmax = sb("nmax", [P, 2, QH])
        ssum = sb("ssum", [P, 2, QH])
        snk = sb("snk", [P, 2, QH])
        cst = sb("cst", [P, 4])
        wg4 = sb("wg4", [P, G4])
        w16 = sb("w16", [P, E])
        e4 = sb("e4", [P, E])
        wts = sb("wts", [P, TOPK, NT])
        row_i = sb("row_i", [P, TOPK * NT], I32)
        ids = sb("ids", [P, TOPK * NT], I32)
        table = sb("table", [P, G4 * E], I32)
        gidx = sb("gidx", [P, G4 * E], I32)
        no_slot = sb("no_slot", [P, G4 * E], I32)
        cnt_i = sb("cnt_i", [P, E], I32)
        icur = sb("icur", [P, 8], I32)
        posi = sb("posi", [P, NT], I32)
        PS = ctx.enter_context(nc.psum_tensor("PS", [P, 8, 512], F32))

        xs = reg0[:, :].rearrange("p (t d) -> p t d", t=NT)
        la = reg0[:, 0:1024].rearrange("p (m s) -> p m s", m=2)
        bb = reg0[:, 1024:2048].rearrange("p (m s) -> p m s", m=2)
        qdec = reg0[:, 2048:3072].rearrange("p (m s) -> p m s", m=2)
        kinv = reg0[:, 3072:4096].rearrange("p (m s) -> p m s", m=2)
        kend = reg1[:, 0:1024].rearrange("p (m s) -> p m s", m=2)
        kend_tm = reg1[:, 1024:2048].rearrange("p (t n) -> p t n", t=NT)
        v = reg23[:, 0:2048].rearrange("p (t n) -> p t n", t=NT)
        S = reg23[:, 2048:4096].rearrange("p (m n e) -> p m n e", m=2, n=NCH)
        rs = reg4[:, :].rearrange("p (h s) -> p h s", h=GH)
        attm = reg5[:, 0:2 * SEQ].rearrange("p (i t s) -> p i t s", i=2, t=NT)
        ada_acc = [reg6[:, 1024 + 512 * i:1536 + 512 * i] for i in range(2)]
        params = reg4[0:R_END, 0:DEPTH * P].rearrange("p (l n) -> p l n", l=DEPTH)
        scanm = reg5[:, 2 * SEQ:3 * SEQ]
        rt = reg1[:, 0:20 * NT * E].rearrange("p (a n) -> p a n", n=NT * E)
        crow = reg7[0:C, 0:P]
        walpha = reg7[0:GLA_RANK, 512:512 + GW]
        lgT = reg7[0:E, 0:512]
        aT = reg7[0:GLA_RANK, 0:512]
        osq = [reg0[:, 512 * h:512 * h + 512] for h in range(GH)]
        orr = [reg7[:, 512 * i:512 * i + 512] for i in range(2)]
        qk = reg6[:, :].rearrange("p (t h d) -> p t h d", t=NT, h=NN)
        sqt = reg1[:, 0:1280]
        qT = reg0[:, 0:2048].rearrange("p (a s) -> p a s", a=QH // 2)
        oTs = reg0[:, 2048:4096].rearrange("p (a s) -> p a s", a=QH // 2)
        kT = reg1[:, 0:1024].rearrange("p (g s) -> p g s", g=KVH)
        kd = reg1[:, 1024:2048].rearrange("p (t g r d) -> p t g r d", t=NT, g=KVH, r=2)
        pT = reg23[:, 0:2048].rearrange("p (b j s) -> p b j s", b=2, j=QH)
        sc = [reg6[:, 0:2048].rearrange("p (j s) -> p j s", j=QH),
              reg23[:, 2048:4096].rearrange("p (j s) -> p j s", j=QH)]
        early = reg5[:, :].rearrange("p (j s) -> p j s", j=C // 2)
        sigb = [r_[:, 0:2048].rearrange("p (j s) -> p j s", j=C // 2) for r_ in (reg1, reg6)]
        mT = reg23[:, :].rearrange("p (j s) -> p j s", j=C)
        otmp = [reg6[:, 512 * i:512 * i + 512] for i in range(2)]
        diag = reg4[:, 0:1024].rearrange("p (c n) -> p c n", c=C)
        xg = [reg23[:, 1024 * i:1024 * i + 1024] for i in range(2)]
        xgT = reg23[:, 3072:4096]
        msig = [reg1[:, 512 * i:512 * i + 512] for i in range(2)]
        mact = [reg1[:, 1024 + 512 * i:1536 + 512 * i] for i in range(2)]
        maT = [reg7[:, 512 * i:512 * i + 512].rearrange("p (f s) -> p f s", f=FC) for i in range(2)]
        ysb = [reg5[:, 1024 * i:1024 * i + 1024] for i in range(2)]
        yc = [r_[:, 2048 * i:2048 * i + 2048].rearrange("p (k d) -> p k d", k=TOPK) for r_ in (reg0, reg23) for i in range(2)]
        o_xg = reg4[:, 0:1024]
        o_sig = reg6[:, 1024:1536]
        o_act = reg6[:, 1536:2048]
        o_aT = reg6[:, 2048:2560].rearrange("p (f s) -> p f s", f=FC)
        o_ysb = reg6[:, 0:1024]

        def slot(u, n=C):
            return ring[:, u % SLOTS, :].rearrange("p (c n) -> p c n", c=n)

        def chunks(flat, c):
            return flat.rearrange("p (c n) -> p c n", c=c)

        def unit_slot(n):
            return UNIT_SLOTS[n % 3]

        half_split = {n: 1024 if n == W_KV else 2048 for n in range(UNITS)}
        unit_chunks = {n: GH if n in (W_UPG, W_UPS) else C for n in range(UNITS)}

        def parts(n):
            size = 2 * half_split[n]
            return tuple(chunks(ring_r[:, i, 0:size], unit_chunks[n]) for i in (2 + n % 2, unit_slot(n)))

        hT_parts = (chunks(ring_r[:, 4, :], C), hT_r[:, :, :])
        rs_parts = (chunks(reg0_r[:, 0:2048], GH), chunks(reg4_r[:, :], GH))
        os_parts = (chunks(reg0_r[:, 0:2048], GH), chunks(reg0_r[:, 2048:4096], GH))
        xgT_parts = (chunks(reg23_r[:, 2048:3072], C), chunks(reg23_r[:, 3072:4096], C))
        gu_high = (hT_r[:, :, :].rearrange("p c s -> p (c s)"), reg0_r[:, :])
        mT_parts = (chunks(ring_r[:, 4, :], C), chunks(reg23_r[:, :], C))

        K = {}

        def counted(name, k):
            s = sem(name)
            K[s.name] = k
            return s

        def at(s, l, k):
            return l * K[s.name] + k

        loaded = [counted(f"slot{i}_loaded", 16 * (BEFORE_MOE[i] + E // 2)) for i in range(SLOTS)]
        small_loaded = counted("small_weights_loaded", 16)
        par_loaded = counted("small_params_loaded", 16 * 4)
        ada_ready = counted("ada_products_ready", ADA)
        ada_summed = counted("ada_columns_ready", ADA)
        diag_done = counted("gate_diagonal_built", 2)
        grow_ready = counted("gate_rows_ready", 2)
        grow_done = counted("gate_rows_copied", 2)
        root = counted("token_rms_rooted", 2)
        hi_done = counted("weight_high_parts_ready", 2 * UNITS)
        lo_done = counted("weight_low_parts_ready", 2 * UNITS)
        a_part = counted("alow_chunk_used", C)
        hx_lo = counted("hT_low_parts_ready", C)
        rs_hi = counted("gla_out_high_ready", 1)
        rs_lo = counted("gla_out_low_ready", 1)
        os_hi = counted("swa_out_high_ready", 1)
        os_lo = counted("swa_out_low_ready", 1)
        m_hi = counted("merged_high_ready", C)
        m_lo = counted("merged_low_ready", C)
        xs_ready = counted("xs_ready", 8)
        ht_ready = counted("hT_ready", 16)
        ht_done = counted("hT_copied", 16)
        scanm_made = counted("scan_mask_made", 2)
        a_done = counted("alow_copied", 1)
        v_ready = counted("v_ready", NT)
        v_done = counted("v_copied", NT)
        u_ready = counted("alpha_ready", 2)
        u_done = counted("alpha_copied", 2)
        labs = counted("alpha_abs_taken", 1)
        lln = counted("log_term_ready", 1)
        b_done = counted("cumsum_ready", 1)
        dif_done = counted("decay_to_end_ready", 1)
        eplus = counted("exponents_ready", 1)
        eend = counted("end_exponents_ready", 1)
        qk_ready = counted("gla_qk_ready", 4)
        qk_done = counted("gla_qk_decayed", 3)
        r_ready = counted("r_ready", 4)
        r_sig = counted("r_sigmoid_ready", 4)
        r_done = counted("r_gated", 4)
        sq_ready = counted("swa_q_ready", NT)
        sq_done = counted("swa_q_copied", NT)
        skv_ready = counted("swa_kv_ready", NT)
        skv_done = counted("swa_kv_copied", NT)
        kt_ready = counted("kend_transposed", 2)
        kt_done = counted("kend_copied", 2)
        kv_ready = counted("kv_ready", 4)
        s_done = counted("states_ready", 1)
        att_ready = counted("att_ready", GH)
        att_done = counted("att_masked", GH)
        o_ready = counted("gla_o_ready", GH)
        osq_done = counted("gla_o_squared", GH)
        ms_ready = counted("gla_mean_square_ready", GH)
        orr_done = counted("gla_root_ready", GH)
        o_done = counted("gla_o_done", GH)
        qsq_done = counted("swa_squares_ready", 2)
        qss_done = counted("swa_square_sums_ready", 2)
        qrt_done = counted("swa_roots_ready", 1)
        rope_done = counted("swa_rotated", 1)
        qT_ready = counted("swa_qT_ready", NT)
        kT_ready = counted("swa_kT_ready", NT)
        qT_done = counted("swa_qT_copied", NT)
        kT_done = counted("swa_kT_copied", NT)
        sc_ready = counted("scores_ready", NT)
        sc_read = counted("scores_read", NT)
        max_done = counted("score_max_ready", NT)
        p_exp = counted("probs_ready", NT)
        p_done = counted("probs_normed", NT)
        pTa_ready = counted("probs_T_ready_act", NT * 2 - 1)
        pTd_ready = counted("probs_T_ready_dve", NT * 2 - 1)
        pTa_done = counted("probs_T_copied_act", NT * 2 - 1)
        pTd_done = counted("probs_T_copied_dve", NT * 2 - 1)
        pv_ready = counted("swa_o_ready", NT)
        pv_done = counted("swa_o_copied", NT)
        mx_ready = counted("mix_products_ready", 4 * C)
        early_done = counted("early_gates_copied", C // 2)
        mx_sig = counted("mix_sigmoids_ready", 2 * C)
        mg_done = counted("gla_up_gated", C)
        mx_done = counted("merged", C)
        out_ready = counted("out_products_ready", 2 * NT)
        x_done = counted("residual_added", 2 * NT)
        xs_out = counted("xs_rows_written", 16)
        lgT_ready = counted("logits_T_ready", 1)
        lgT_done = counted("logits_T_copied", 1)
        lg_ready = counted("logits_ready", 1)
        aff_done = counted("affinities_ready", 1)
        m_done = counted("choice_mask_ready", 1)
        rk_ready = counted("ranks_ready", 1)
        row_done = counted("table_rows_ready", 1)
        tab_clear = counted("table_cleared", 16)
        tab_set = counted("table_filled", 16 * TOPK * NT)
        tab_loaded = counted("table_loaded", 16)
        idx_done = counted("gather_rows_ready", 1)
        gcur_done = counted("gather_column_copied", E)
        dcur_done = counted("scatter_column_copied", E)
        xg_loaded = [counted(f"expert_tokens_gathered_{i}", 8 * E) for i in range(2)]
        t1_ready = counted("expert_tokens_transposed", E)
        x_hi = counted("expert_tokens_high_ready", E)
        x_lo = counted("expert_tokens_low_ready", E)
        gu_hi = [counted(f"expert_{n}_high_ready", 2 * E) for n in ("gate", "up")]
        gu_lo = [counted(f"expert_{n}_low_ready", 2 * E) for n in ("gate", "up")]
        g_ready = counted("gate_product_ready", E)
        u2_ready = counted("up_product_ready", E)
        gu_free = counted("gate_up_weights_free", E)
        sig_done = counted("gate_sigmoid_ready", E)
        act_done = counted("expert_act_ready", E)
        t2_ready = counted("expert_act_transposed", E)
        t2_done = counted("expert_act_copied", E)
        d_ready = counted("down_product_ready", E)
        y_done = counted("expert_y_ready", E + 1)
        y_stored = [counted(f"expert_y_scattered_{i}", 8 * E) for i in range(2)]
        yc_loaded = [counted(f"chosen_y_loaded_{i}", 16) for i in range(NT)]
        x2_done = counted("moe_added", NT)
        x_loaded = sem("x_loaded")
        const_loaded = sem("constants_loaded")
        pool_consts = sem("pool_constants")
        dve_consts = sem("dve_constants")
        trig = sem("trig_steps")
        trig_act = sem("trig_functions")
        cond_t = sem("condition_transposed")
        pcs_ready = sem("parameters_transposed")
        cond_sig = sem("condition_sigmoid")
        cond_done = sem("condition_ready")
        x_stored = sem("x_stored")
        o_icur = sem("ovf_index_copied")
        o_gath = sem("ovf_gathered")
        o_t1 = sem("ovf_tokens_transposed")
        o_t1c = sem("ovf_tokens_copied")
        o_xl = sem("ovf_tokens_low_ready")
        o_gu = sem("ovf_gate_up_ready")
        o_sg = sem("ovf_sigmoid_ready")
        o_ac = sem("ovf_act_ready")
        o_t2 = sem("ovf_act_transposed")
        o_t2c = sem("ovf_act_copied")
        o_d = sem("ovf_down_ready")
        o_y = sem("ovf_y_ready")
        o_st = sem("ovf_scattered")

        used = {W_SQ: (sq_ready, NT), W_KV: (skv_ready, NT), W_V: (v_ready, NT), W_QK: (qk_ready, 4),
                W_R: (r_ready, 4), W_MA0: (mx_ready, 4), W_MA1: (mx_ready, 8), W_UPG: (mx_ready, 16),
                W_MB0: (mx_ready, 20), W_MB1: (mx_ready, 24), W_UPS: (mx_ready, 32),
                W_O0: (out_ready, NT), W_O1: (out_ready, 2 * NT)}

        def unit_loaded(n):
            return loaded[unit_slot(n)], 16 * (ADA // SLOTS + n // 3 + 1)

        block = ctx.enter_context(nc.Block())

        def overflow_blocks(eng, e, done, body):
            count = eng.value_load(cnt_i[0:1, bass.ds(e, 1)], min_val=0, max_val=SEQ)
            for b in range(1, NT):
                with eng.If(count > P * b):
                    eng.reg_add(done, done, 1)
                    body(b, eng.snap(done, min_val=1, max_val=4096))
                    eng.nop()

        @block.sync
        def _(sp):
            def load_ada(l, u):
                sp.dma_start(slot(u), w_ada[l, :, 512 * u:512 * u + 512].rearrange("(c p) n -> p c n", p=P)).then_inc(loaded[u % SLOTS], 16)

            def load(l, n):
                size = 2 * half_split[n]
                if n in (W_UPG, W_UPS):
                    src = (w_up_gla if n == W_UPG else w_up_swa)[l]
                elif n in (W_O0, W_O1):
                    src = w_out[l, :, 512 * (n - W_O0):512 * (n - W_O0) + 512]
                else:
                    at_col = {W_SQ: col_sq, W_KV: col_sk, W_V: col_v, W_QK: col_qk, W_R: col_r, W_MA0: col_ma,
                              W_MA1: col_ma + 512, W_MB0: col_mb, W_MB1: col_mb + 512}[n]
                    src = w_in[l, :, at_col:at_col + size // C]
                sp.dma_start(ring[:, unit_slot(n), 0:size].rearrange("p (c n) -> p c n", c=unit_chunks[n]),
                             src.rearrange("(c p) n -> p c n", p=P)).then_inc(loaded[unit_slot(n)], 16)

            def load_expert(l, e, k, part):
                u = 3 * k + part
                src = (w_gate, w_up, w_down)[part][l, e].rearrange("(c p) n -> p c n", p=P)
                sp.dma_start(slot(u, src.shape[1]), src).then_inc(loaded[u % SLOTS], 16)

            sp.dma_start(crow, c.rearrange("b (c p) -> (b c) p", p=P)).then_inc(const_loaded, 16)
            load_ada(0, 0)
            sp.dma_start(posi[:, :], positions.rearrange("b (t p) -> p (b t)", p=P),
                         allow_slow_non_contiguous=True).then_inc(const_loaded, 16)
            sp.dma_start(wr[:, :, :], w_router.rearrange("(c p) e -> p c e", p=P)).then_inc(const_loaded, 16)
            sp.dma_start(br[:, :], b_router.rearrange("(a e) -> a e", a=1).broadcast_to([P, E])).then_inc(const_loaded, 16)
            for a, b, src in ((R_SH1, R_NM, b_ada), (R_NM, R_NF, norm_mix), (R_NF, R_BA, norm_ffn),
                              (R_BA, R_GN, b_alpha), (R_GN, R_END, gla_norm)):
                sp.dma_start(params[a:b, :, :], src.rearrange("l (c p) -> c l p", p=P)).then_inc(const_loaded, 16)
            for u in range(1, SLOTS):
                load_ada(0, u)
            sp.dma_start(xt[:, :, :], x[0].rearrange("(t p) d -> p t d", p=P)).then_inc(x_loaded, 16)
            number = sp.alloc_register("sp_wait_value")

            def in_register(value):
                sp.reg_mov(number, value)
                return sp.snap(number, min_val=1, max_val=1 << 14)

            def wait(s, value):
                value = in_register(value)
                sp.wait_ge(const_loaded, 16 * 9)
                sp.wait_ge(s, value)

            with sp.Fori(0, DEPTH) as l:
                sp.dma_start(w_a[:, :, :], w_in[l, :, col_a:col_a + GLA_RANK].rearrange("(c p) n -> p c n", p=P)).then_inc(small_loaded, 16)
                for u in range(SLOTS):
                    wait(ada_summed, at(ada_summed, l, u + 1))
                    load_ada(l, u + SLOTS)
                for n, u in enumerate((0, 1, 5)):
                    wait(ada_summed, at(ada_summed, l, SLOTS + u + 1))
                    load(l, n)
                for n in range(UNITS - 3):
                    wait(used[n][0], at(used[n][0], l, used[n][1]))
                    load(l, n + 3)
                wait(used[W_UPS][0], at(used[W_UPS][0], l, used[W_UPS][1]))
                load_expert(l, 0, 0, 1)
                wait(out_ready, at(out_ready, l, NT))
                load_expert(l, 1, 1, 0)
                load_expert(l, 1, 1, 2)
                wait(out_ready, at(out_ready, l, 2 * NT))
                for e, part in ((0, 0), (0, 2), (1, 1)):
                    load_expert(l, e, e, part)

                def load_gate_up(e, k):
                    for part in range(2):
                        sp.wait_ge(gu_free, at(gu_free, l, e - 1))
                        load_expert(l, e, k, part)

                def load_down(e, k):
                    sp.wait_ge(d_ready, at(d_ready, l, e - 1))
                    load_expert(l, e, k, 2)

                load_gate_up(2, 0)
                with sp.Fori(0, E // 2 - 2) as j:
                    for k in range(2):
                        load_gate_up(2 * j + (3 + k), 1 - k)
                        load_down(2 * j + (2 + k), k)
                load_gate_up(E - 1, 1)
                load_down(E - 2, 0)
                load_down(E - 1, 1)
                with sp.If(l < DEPTH - 1):
                    following = nc.s_assert_within(l + 1, 1, DEPTH - 1, skip_runtime_bounds_check_because="the If above bounds it")
                    for u in range(SLOTS):
                        s = d_ready if u % 3 == 2 else gu_free
                        sp.wait_ge(s, at(s, l, E - 1 + u // 3))
                        load_ada(following, u)
                sp.nop()
            for t in range(NT):
                sp.wait_ge(x2_done, at(x2_done, DEPTH - 1, t + 1))
                sp.dma_start(out[0, t * P:t * P + P, :], xt[:, t, :]).then_inc(x_stored, 16)
            sp.wait_ge(x_stored, 16 * NT)

        @block.gpsimd
        def _(pool):
            pool.memset(ident[:, :], 0.0).then_inc(pool_consts, 1)
            pool.memset(ones[:, :], 1.0).then_inc(pool_consts, 1)
            pool.memset(band[:, :], 0.0).then_inc(pool_consts, 1)
            pool.memset(no_slot[:, :], 4 * SEQ).then_inc(pool_consts, 1)
            pool.iota(ids[:, :].rearrange("p (k t) -> p k t", k=TOPK), [[1, TOPK], [2 * P, NT]], base=0,
                      channel_multiplier=2).then_inc(pool_consts, 1)
            pool.wait_ge(pool_consts, 5)
            pool.affine_select(out=ident[:, :], in_=ident[:, :], compare_op=ALU.not_equal, fill=1.0, base=0,
                               pattern=[[-1, P]], channel_multiplier=1).then_inc(pool_consts, 1)
            pool.affine_select(out=before[:, :], in_=ones[:, :], compare_op=ALU.is_gt, fill=0.0, base=0,
                               pattern=[[1, P]], channel_multiplier=-1).then_inc(pool_consts, 1)
            pool.affine_select(out=causal[:, :], in_=ones[:, :], compare_op=ALU.is_ge, fill=0.0, base=0,
                               pattern=[[1, P]], channel_multiplier=-1).then_inc(pool_consts, 1)
            pool.affine_select(out=band[:, :], in_=band[:, :], compare_op=ALU.is_gt, fill=NEG, base=0,
                               pattern=[[1, 2 * P]], channel_multiplier=-1).then_inc(pool_consts, 1)
            pool.wait_ge(pool_consts, 9)
            pool.affine_select(out=band[:, :], in_=band[:, :], compare_op=ALU.is_ge, fill=NEG, base=P,
                               pattern=[[-1, 2 * P]], channel_multiplier=1).then_inc(pool_consts, 1)
            pool.memset(causal[0:CHUNK, CHUNK:P], 0.0).then_inc(pool_consts, 1)
            for tile, pattern, base in ((wg4, [[-1, G4]], G4), (w16, [[-1, E]], E), (e4, [[G4, E]], 0)):
                pool.iota(tile[:, :], pattern, base=base, channel_multiplier=0,
                          allow_small_or_imprecise_dtypes=True).then_inc(pool_consts, 1)

            done = pool.alloc_register("pool_ovf")
            pool.reg_mov(done, 0)
            number = pool.alloc_register("pool_wait_value")

            def in_register(value):
                pool.reg_mov(number, value)
                return pool.snap(number, min_val=1, max_val=1 << 14)

            pool.wait_ge(const_loaded, 16 * 9)

            with pool.Fori(0, DEPTH) as l:
                pool.dma_start(walpha, w_alpha2[l]).then_inc(par_loaded, 16)
                pool.dma_start(gains[:, 0, :], q_norm[bass.ds(l, 1), :].broadcast_to([P, HD])).then_inc(par_loaded, 16)
                pool.dma_start(gains[:, 1, :], k_norm[bass.ds(l, 1), :].broadcast_to([P, HD])).then_inc(par_loaded, 16)
                pool.memset(scanm, 1.0).then_inc(scanm_made, 1)
                value = in_register(at(scanm_made, l, 1))
                pool.wait_ge(pool_consts, 14)
                pool.wait_ge(scanm_made, value)
                pool.memset(scanm.rearrange("p (n s) -> p n s", s=CHUNK)[:, :, 0:1], 0.0).then_inc(scanm_made, 1)
                pool.dma_start(sink_t[:, :], sinks[bass.ds(l, 1), :].broadcast_to([P, QH])).then_inc(par_loaded, 16)
                pool.dma_start(slot_table.rearrange("(p n) a -> p (n a)", p=P), no_slot[:, :]).then_inc(tab_clear, 16)
                value = in_register(at(xs_ready, l, 2 * NT))
                pool.wait_ge(pool_consts, 14)
                pool.wait_ge(xs_ready, value)
                pool.dma_start(xs_rows.rearrange("(t p) d -> p t d", p=P), xs).then_inc(xs_out, 16)
                values = [in_register(at(tab_clear, l, 16)), in_register(at(row_done, l, 1))]
                pool.wait_ge(pool_consts, 14)
                pool.wait_ge(tab_clear, values[0])
                pool.wait_ge(row_done, values[1])
                for i in range(TOPK * NT):
                    pool.indirect_dma_start(out=slot_table[:, :], out_offset=bass.IndirectOffsetOnAxis(
                        ap=row_i[:, i:i + 1].bitcast(U32), axis=0), in_=ids[:, i:i + 1], in_offset=None).then_inc(tab_set, 16)
                value = in_register(at(tab_set, l, 16 * TOPK * NT))
                pool.wait_ge(pool_consts, 14)
                pool.wait_ge(tab_set, value)
                pool.dma_start(table[:, :], slot_table.rearrange("(p n) a -> p (n a)", p=P)).then_inc(tab_loaded, 16)
                values = [in_register(at(idx_done, l, 1)), in_register(at(xs_out, l, 16))]
                pool.wait_ge(pool_consts, 14)
                pool.wait_ge(idx_done, values[0])
                pool.wait_ge(xs_out, values[1])

                def gather(e, k):
                    pool.tensor_copy(icur[:, k:k + 1], gidx[:, bass.ds(e * G4, 1)]).then_inc(gcur_done, 1)
                    value = in_register(at(gcur_done, l, e + 1))
                    pool.wait_ge(pool_consts, 14)
                    pool.wait_ge(gcur_done, value)
                    pool.indirect_dma_start(out=xg[k], out_offset=None, in_=xs_rows[:, :],
                                            in_offset=bass.IndirectOffsetOnAxis(ap=icur[:, k:k + 1].bitcast(U32), axis=0)).then_inc(xg_loaded[k], 16)

                def scatter(e, k):
                    value = in_register(at(y_done, l, e + 2))
                    pool.wait_ge(pool_consts, 14)
                    pool.wait_ge(y_done, value)
                    pool.tensor_copy(icur[:, 2 + k:3 + k], table[:, bass.ds(e * G4, 1)]).then_inc(dcur_done, 1)
                    value = in_register(at(dcur_done, l, e + 1))
                    pool.wait_ge(pool_consts, 14)
                    pool.wait_ge(dcur_done, value)
                    pool.indirect_dma_start(out=y_rows[:, :], out_offset=bass.IndirectOffsetOnAxis(
                        ap=icur[:, 2 + k:3 + k].bitcast(U32), axis=0), in_=ysb[k], in_offset=None,
                        bounds_check=TOPK * SEQ - 1, oob_is_err=False).then_inc(y_stored[k], 16)

                def overflow(e):
                    def body(b, n):
                        pool.tensor_copy(icur[:, 4:5], gidx[:, bass.ds(e * G4 + b, 1)]).then_inc(o_icur, 1)
                        pool.tensor_copy(icur[:, 5:6], table[:, bass.ds(e * G4 + b, 1)]).then_inc(o_icur, 1)
                        value = in_register(2 * n)
                        pool.wait_ge(pool_consts, 14)
                        pool.wait_ge(o_icur, value)
                        pool.indirect_dma_start(out=o_xg, out_offset=None, in_=xs_rows[:, :],
                                                in_offset=bass.IndirectOffsetOnAxis(ap=icur[:, 4:5].bitcast(U32), axis=0)).then_inc(o_gath, 16)
                        value = n
                        pool.wait_ge(pool_consts, 14)
                        pool.wait_ge(o_y, value)
                        pool.indirect_dma_start(out=y_rows[:, :], out_offset=bass.IndirectOffsetOnAxis(
                            ap=icur[:, 5:6].bitcast(U32), axis=0), in_=o_ysb, in_offset=None,
                            bounds_check=TOPK * SEQ - 1, oob_is_err=False).then_inc(o_st, 16)
                        value = in_register(16 * n)
                        pool.wait_ge(pool_consts, 14)
                        pool.wait_ge(o_st, value)
                    overflow_blocks(pool, e, done, body)

                def gather_next(e, k):
                    value = in_register(at(t1_ready, l, e + 1))
                    pool.wait_ge(pool_consts, 14)
                    pool.wait_ge(t1_ready, value)
                    gather(e + 2, k)

                gather(0, 0)
                gather(1, 1)
                gather_next(0, 0)
                overflow(0)
                gather_next(1, 1)

                def step(s, k, more=True):
                    overflow(s)
                    scatter(s - 1, 1 - k)
                    if more:
                        gather_next(s + 1, 1 - k)

                with pool.Fori(0, E // 2 - 2) as j:
                    step(2 * j + 1, 1)
                    step(2 * j + 2, 0)
                for e in range(E - 3, E):
                    step(e, e % 2, more=False)
                scatter(E - 1, 1)
                values = [in_register(at(y_stored[i], l, 8 * E)) for i in range(2)]
                pool.wait_ge(pool_consts, 14)
                for i in range(2):
                    pool.wait_ge(y_stored[i], values[i])
                for t in range(NT):
                    pool.dma_start(yc[t], y_rows[2 * P * t:2 * P * (t + 1), :].rearrange("(p k) d -> p k d", k=TOPK)).then_inc(yc_loaded[t], 16)
                value = in_register(at(x2_done, l, NT))
                pool.wait_ge(pool_consts, 14)
                pool.wait_ge(x2_done, value)

        @block.scalar
        def _(act):
            done = act.alloc_register("act_ovf")
            act.reg_mov(done, 0)
            act.wait_ge(cond_t, 1)
            act.activation(a1[:, :], PS[:, 2, 0:C], ACT.Sigmoid).then_inc(cond_sig, 1)
            act.wait_ge(trig, 1)
            act.activation(sinr[:, :, :], sinr[:, :, :], ACT.Sin)
            act.activation(cosr[:, :, :], cosr[:, :, :], ACT.Sin).then_inc(trig_act, 1)
            act.wait_ge(x_loaded, 16)
            act.wait_ge(dve_consts, 1)
            eps, one = cst[:, 0:1], cst[:, 1:2]

            with act.Fori(0, DEPTH) as l:
                def norm_tokens(r):
                    for t in range(NT):
                        if r == 1:
                            act.wait_ge(x_done, at(x_done, l, NT + t + 1))
                        act.activation(hT[:, 2 * t:2 * t + 2, :], xt[:, t, :].rearrange("p (a s) -> p a s", a=2), ACT.Square,
                                       accum_out=ss[:, t:t + 1])
                    act.drain()
                    act.activation(ss[:, :], ss[:, :], ACT.Sqrt, scale=1.0 / D, bias=eps).then_inc(root, 1)

                def copy_hT(r, scale, shift):
                    for k in range(C):
                        act.wait_ge(ht_ready, at(ht_ready, l, C * r + k + 1))
                        if r == 0:
                            act.activation(hT_parts[0][:, k, :], PS[:, k, :], ACT.Identity, scale=scale[:, k:k + 1],
                                           bias=shift[:, k:k + 1])
                        act.activation(hT[:, k, :], PS[:, k, :], ACT.Identity, scale=scale[:, k:k + 1],
                                       bias=shift[:, k:k + 1]).then_inc(ht_done, 1)

                def split_high(n):
                    s, value = unit_loaded(n)
                    act.wait_ge(s, at(s, l, value))
                    if n < 2:
                        act.wait_ge(ada_summed, at(ada_summed, l, SLOTS + 3 + n))
                    else:
                        act.wait_ge(used[n - 2][0], at(used[n - 2][0], l, used[n - 2][1]))
                    for h in range(2):
                        cols = slice(half_split[n] * h, half_split[n] * (h + 1))
                        act.activation(ring_r[:, 2 + n % 2, cols], ring[:, unit_slot(n), cols], ACT.Copy).then_inc(hi_done, 1)

                def copy_grow(r, bank):
                    act.wait_ge(grow_ready, at(grow_ready, l, r + 1))
                    act.activation(grow[:, :].rearrange("p (a s) -> p a s", a=2), PS[:, bank:bank + 2, :], ACT.Copy).then_inc(grow_done, 1)

                norm_tokens(0)
                split_high(0)
                split_high(1)
                act.wait_ge(diag_done, at(diag_done, l, 1))
                copy_hT(0, a1, pc[:, R_SH1:R_SH1 + C])
                act.wait_ge(a_part, at(a_part, l, C))
                act.activation(aT, PS[0:GLA_RANK, 0, :], ACT.Copy).then_inc(a_done, 1)
                for t in range(NT):
                    act.wait_ge(sq_ready, at(sq_ready, l, t + 1))
                    act.activation(qk[:, t, 0:QH, :], PS[:, 2 + t, :].rearrange("p (h d) -> p h d", d=HD), ACT.Copy).then_inc(sq_done, 1)
                split_high(2)
                for t in range(NT):
                    act.wait_ge(skv_ready, at(skv_ready, l, t + 1))
                    b = (6 + t) % 8
                    act.activation(qk[:, t, QH:NN, :], PS[:, b, 0:KVH * HD].rearrange("p (h d) -> p h d", d=HD), ACT.Copy)
                    act.activation(v_tm[:, t, :], PS[:, b, KVH * HD:2 * KVH * HD], ACT.Copy).then_inc(skv_done, 1)
                split_high(3)
                act.drain()
                for i in range(2):
                    if i == 1:
                        act.wait_ge(qss_done, at(qss_done, l, 1))
                    act.activation(sqt, qk[:, 2 * i:2 * i + 2, :, :].rearrange("p t h d -> p (t h d)"), ACT.Square).then_inc(qsq_done, 1)
                act.wait_ge(qss_done, at(qss_done, l, 2))
                act.activation(qss[:, :, :], qss[:, :, :], ACT.Sqrt, scale=1.0 / HD, bias=eps).then_inc(qrt_done, 1)
                for t in range(NT):
                    act.wait_ge(v_ready, at(v_ready, l, t + 1))
                    act.activation(v[:, t, :], PS[:, 2 + t, :], ACT.Copy).then_inc(v_done, 1)
                split_high(4)
                for m in range(2):
                    act.wait_ge(u_ready, at(u_ready, l, m + 1))
                    act.activation(la[:, m, :], PS[:, 6 + m, :], ACT.Identity, bias=pc[:, R_BA + m:R_BA + m + 1]).then_inc(u_done, 1)
                copy_grow(0, 0)
                act.drain()
                act.activation(bb, la, ACT.Abs).then_inc(labs, 1)
                act.drain()
                act.activation(bb, bb, ACT.Exp, scale=-1.0)
                act.drain()
                act.activation(bb, bb, ACT.Ln, bias=one).then_inc(lln, 1)
                act.wait_ge(b_done, at(b_done, l, 1))
                act.activation(qdec, bb, ACT.Exp, scale=1.0 / GLA_TAU)
                act.activation(decay[:, :, :], bb.rearrange("p m (n s) -> p m n s", s=CHUNK)[:, :, :, CHUNK - 1], ACT.Exp,
                               scale=1.0 / GLA_TAU)
                act.activation(kinv, bb, ACT.Exp, scale=-1.0 / GLA_TAU).then_inc(eplus, 1)
                act.wait_ge(dif_done, at(dif_done, l, 1))
                act.activation(kend, la, ACT.Exp, scale=-1.0 / GLA_TAU).then_inc(eend, 1)
                split_high(5)
                for m in range(GH):
                    act.wait_ge(r_ready, at(r_ready, l, m + 1))
                    act.activation(rs[:, m, :], PS[:, (6 + m) % 8, :], ACT.Sigmoid).then_inc(r_sig, 1)
                split_high(6)
                for h in range(GH):
                    act.wait_ge(o_ready, at(o_ready, l, h + 1))
                    act.activation(osq[h], PS[:, 4 + h, :], ACT.Square).then_inc(osq_done, 1)
                for h in range(GH):
                    act.wait_ge(ms_ready, at(ms_ready, l, h + 1))
                    if h >= 2:
                        act.wait_ge(o_done, at(o_done, l, h - 1))
                    act.activation(orr[h % 2], PS[:, h, :], ACT.Sqrt, scale=1.0 / P, bias=eps).then_inc(orr_done, 1)
                for t in range(NT):
                    act.wait_ge(qT_ready, at(qT_ready, l, t + 1))
                    act.activation(qT[:, :, t * P:t * P + P], PS[:, t, :].rearrange("p (a s) -> p a s", s=P), ACT.Copy).then_inc(qT_done, 1)
                for n in range(NT):
                    lo = P if n == 0 else 0
                    act.wait_ge(max_done, at(max_done, l, n + 1))
                    act.activation(snk[:, n % 2, :], snk[:, n % 2, :], ACT.Exp)
                    for j in range(QH):
                        a = act.activation(sc[n % 2][:, j, lo:], sc[n % 2][:, j, lo:], ACT.Exp, bias=nmax[:, n % 2, j:j + 1],
                                           accum_out=ssum[:, n % 2, j:j + 1])
                    a.then_inc(p_exp, 1)
                    act.wait_ge(mx_ready, at(mx_ready, l, n + 1))
                    act.activation(early[:, n, :], PS[:, 5, :], ACT.Copy).then_inc(early_done, 1)
                    for b in range(1 if n == 0 else 0, 2):
                        i = 2 * n + b - 1
                        act.wait_ge(pTa_ready, at(pTa_ready, l, i + 1))
                        act.activation(pT[:, b, 0:4, :], PS[:, 4, :].rearrange("p (j s) -> p j s", s=P), ACT.Copy).then_inc(pTa_done, 1)
                    act.wait_ge(pv_ready, at(pv_ready, l, n + 1))
                    act.activation(oTs[:, :, n * P:n * P + P], PS[:, 7, :].rearrange("p (a s) -> p a s", s=P), ACT.Copy).then_inc(pv_done, 1)
                act.wait_ge(o_done, at(o_done, l, GH))
                act.activation(rs_parts[0].rearrange("p h s -> p (h s)"), reg4[:, :], ACT.Copy).then_inc(rs_hi, 1)

                def gate_sigmoids(first, products, dst, j0):
                    for j in range(j0, j0 + C // 2):
                        act.wait_ge(mx_ready, at(mx_ready, l, products + j + 1))
                        act.activation(dst[:, j - first, :], PS[:, j, :], ACT.Sigmoid).then_inc(mx_sig, 1)

                act.drain()
                for j in range(C // 2):
                    act.activation(mT[:, j, :], early[:, j, :], ACT.Sigmoid).then_inc(mx_sig, 1)
                split_high(W_UPG)
                gate_sigmoids(0, 0, mT, C // 2)
                split_high(W_MB0)
                act.wait_ge(mx_ready, at(mx_ready, l, 2 * C))
                act.activation(os_parts[0].rearrange("p h s -> p (h s)"), reg0[:, 2048:4096], ACT.Copy).then_inc(os_hi, 1)
                split_high(W_MB1)
                gate_sigmoids(0, 2 * C, sigb[0], 0)
                split_high(W_UPS)
                gate_sigmoids(C // 2, 2 * C, sigb[1], C // 2)
                split_high(W_O0)
                for j in range(C):
                    act.wait_ge(mx_done, at(mx_done, l, j + 1))
                    act.activation(mT_parts[0][:, j, :], mT[:, j, :], ACT.Copy).then_inc(m_hi, 1)
                split_high(W_O1)
                norm_tokens(1)
                copy_hT(1, a2, pc[:, R_SH2:R_SH2 + C])
                act.wait_ge(lgT_ready, at(lgT_ready, l, 1))
                act.activation(lgT, PS[0:E, 0, :], ACT.Copy).then_inc(lgT_done, 1)
                act.wait_ge(lg_ready, at(lg_ready, l, 1))
                act.activation(rt[:, 0, :], PS[:, 1, 0:NT * E], ACT.Sigmoid).then_inc(aff_done, 1)
                copy_grow(1, 3)

                def token_parts():
                    for k in range(C):
                        act.activation(xgT[:, k * P:k * P + P], PS[:, 2 + k // 4, P * (k % 4):P * (k % 4) + P], ACT.Identity,
                                       scale=a2[:, k:k + 1], bias=pc[:, R_SH2 + k:R_SH2 + k + 1])
                    act.drain()
                    return act.activation(xgT_parts[0].rearrange("p c s -> p (c s)"), xgT, ACT.Copy)

                def tokens(e):
                    act.wait_ge(t1_ready, at(t1_ready, l, e + 1))
                    token_parts().then_inc(x_hi, 1)

                def weights_high(e, pair, k, part):
                    s = loaded[3 * k + part]
                    act.wait_ge(s, at(s, l, 16 * (BEFORE_MOE[3 * k + part] + 1) + 16 * pair))
                    for h in range(2):
                        cols = slice(2048 * h, 2048 * h + 2048)
                        act.activation(gu_high[part][:, cols], ring[:, 3 * k + part, cols], ACT.Copy).then_inc(gu_hi[part], 1)

                def gate(e, k):
                    act.wait_ge(g_ready, at(g_ready, l, e + 1))
                    act.activation(msig[k], PS[:, 0, :], ACT.Sigmoid).then_inc(sig_done, 1)

                def hidden(e, k):
                    act.wait_ge(t2_ready, at(t2_ready, l, e + 1))
                    act.activation(maT[k], PS[:, 4, :].rearrange("p (f s) -> p f s", s=P), ACT.Copy).then_inc(t2_done, 1)

                def overflow(e):
                    def body(b, n):
                        act.wait_ge(o_t1, n)
                        token_parts().then_inc(o_t1c, 1)
                        act.wait_ge(o_gu, n)
                        act.activation(o_sig, PS[:, 0, :], ACT.Sigmoid).then_inc(o_sg, 1)
                        act.wait_ge(o_t2, n)
                        act.activation(o_aT, PS[:, 4, :].rearrange("p (f s) -> p f s", s=P), ACT.Copy).then_inc(o_t2c, 1)
                    overflow_blocks(act, e, done, body)

                weights_high(0, 0, 0, 0)
                act.wait_ge(xs_out, at(xs_out, l, 16))
                weights_high(0, 0, 0, 1)
                act.wait_ge(row_done, at(row_done, l, 1))
                tokens(0)

                def step(s, pair_after, k):
                    gate(s, k)
                    overflow(s)
                    if pair_after is not None:
                        weights_high(s + 1, pair_after, 1 - k, 0)
                    if not isinstance(s, int) or s > 0:
                        hidden(s - 1, 1 - k)
                    if pair_after is not None:
                        tokens(s + 1)
                        act.wait_ge(u2_ready, at(u2_ready, l, s + 1))
                        weights_high(s + 1, pair_after, 1 - k, 1)

                step(0, 0, 0)
                with act.Fori(0, E // 2 - 1) as j:
                    step(2 * j + 1, j + 1, 1)
                    step(2 * j + 2, j + 1, 0)
                step(E - 1, None, 1)
                hidden(E - 1, 1)
                act.wait_ge(x2_done, at(x2_done, l, NT))

        @block.tensor
        def _(pe):
            done = pe.alloc_register("pe_ovf")
            pe.reg_mov(done, 0)
            pe.wait_ge(pool_consts, 11)
            pe.wait_ge(const_loaded, 16 * 9)
            pe.transpose(PS[:, 2, 0:C], crow, ident[0:C, 0:C]).then_inc(cond_t, 1)
            for i in range(DEPTH):
                mm = pe.transpose(PS[:, 3, i * R_END:i * R_END + R_END], params[:, i, :], ident[0:R_END, 0:R_END])
            mm.then_inc(pcs_ready, 1)
            pe.wait_ge(cond_done, 1)

            def condition_products(l, units):
                for u in units:
                    pe.wait_ge(loaded[u % SLOTS], at(loaded[u % SLOTS], l, 16 * (u // SLOTS + 1)))
                    for i in range(4):
                        for k in range(ADA_DVE, C):
                            pe.matmul(PS[:, 7, 4 * u + i:4 * u + i + 1], slot(u)[:, k, i * P:i * P + P], condT[:, k:k + 1],
                                      start=(u == units[0] and i == 0 and k == ADA_DVE), stop=False, skip_group_check=True)

            def condition_sums(l, units):
                for u in units:
                    pe.wait_ge(ada_ready, at(ada_ready, l, u + 1))
                    for i in range(4):
                        mm = pe.matmul(PS[:, 7, 4 * u + i:4 * u + i + 1], ada_acc[u % 2][:, i * P:i * P + P], ones[:, 0:1],
                                       start=False, stop=True, skip_group_check=True)
                    mm.then_inc(ada_summed, 1)

            for u in range(ADA_EARLY):
                condition_products(0, [u])
                condition_sums(0, [u])
            with pe.Fori(0, DEPTH) as l:
                def wait_unit(n):
                    pe.wait_ge(lo_done, at(lo_done, l, 2 * n + 2))

                def gate_rows(r, bank):
                    pe.wait_ge(diag_done, at(diag_done, l, r + 1))
                    for h in range(2):
                        mm = pe.matmul(PS[:, bank + h, :], ones[:, :], diag[:, 4 * h:4 * h + 4, :], start=True, stop=True)
                    mm.then_inc(grow_ready, 1)

                def transpose_tokens(chunks_):
                    for k in chunks_:
                        for t in range(NT):
                            mm = pe.transpose(PS[:, k, t * P:t * P + P], xs[:, t, k * P:k * P + P], ident[:, :])
                        mm.then_inc(ht_ready, 1)

                condition_products(l, [ADA_EARLY])
                condition_sums(l, [ADA_EARLY])
                condition_products(l, range(ADA_EARLY + 1, ADA))
                pe.wait_ge(xs_ready, at(xs_ready, l, NT))
                transpose_tokens(range(7))
                condition_sums(l, range(ADA_EARLY + 1, ADA))
                pe.wait_ge(diag_done, at(diag_done, l, 1))
                transpose_tokens(range(7, C))

                def three_passes(out_, left, right, first, last):
                    pe.matmul(out_, left[0], right[0], start=first, stop=False)
                    pe.matmul(out_, left[0], right[1], start=False, stop=False)
                    return pe.matmul(out_, left[1], right[0], start=False, stop=last)

                def channel_major(bank, n, cols, x_parts=hT_parts):
                    w, depth = parts(n), unit_chunks[n]
                    for k in range(depth):
                        mm = three_passes(PS[:, bank, :], [a[:, k, cols] for a in w], [a[:, k, :] for a in x_parts],
                                          k == 0, k == depth - 1)
                    return mm

                def token_major(bank, t, n, width, x_parts=hT_parts, chunk_ready=None):
                    w = parts(n)
                    for k in range(C):
                        if chunk_ready is not None:
                            pe.wait_ge(chunk_ready, at(chunk_ready, l, k + 1))
                        mm = three_passes(PS[:, bank, 0:width], [a[:, k, t * P:t * P + P] for a in x_parts],
                                          [a[:, k, :] for a in w], k == 0, k == C - 1)
                    return mm

                pe.wait_ge(small_loaded, at(small_loaded, l, 16))
                pe.wait_ge(ht_done, at(ht_done, l, 1))
                for k in range(C):
                    if k > 0:
                        pe.wait_ge(ht_done, at(ht_done, l, k + 1))
                    pe.matmul(PS[0:GLA_RANK, 0, :], w_a[:, k, :], hT[:, k, :], start=(k == 0), stop=(k == C - 1)).then_inc(a_part, 1)
                pe.wait_ge(hx_lo, at(hx_lo, l, C))
                wait_unit(W_SQ)
                for t in range(NT):
                    token_major(2 + t, t, W_SQ, QH * HD).then_inc(sq_ready, 1)
                wait_unit(W_KV)
                pe.wait_ge(a_done, at(a_done, l, 1))
                for t in range(NT):
                    token_major((6 + t) % 8, t, W_KV, 2 * KVH * HD).then_inc(skv_ready, 1)
                wait_unit(W_V)
                pe.wait_ge(sq_done, at(sq_done, l, NT))
                for t in range(NT):
                    token_major(2 + t, t, W_V, GV).then_inc(v_ready, 1)
                pe.wait_ge(par_loaded, at(par_loaded, l, 16 * 4))
                pe.wait_ge(skv_done, at(skv_done, l, NT))
                for m in range(2):
                    pe.matmul(PS[:, 6 + m, :], walpha[:, m * P:m * P + P], aT, start=True, stop=True).then_inc(u_ready, 1)
                gate_rows(0, 0)
                wait_unit(W_QK)
                for m in range(4):
                    pe.wait_ge(v_done, at(v_done, l, m + 1))
                    channel_major(2 + m, W_QK, slice(m * P, m * P + P)).then_inc(qk_ready, 1)
                wait_unit(W_R)
                pe.wait_ge(u_done, at(u_done, l, 2))
                for h in range(GH):
                    if h == 2:
                        pe.wait_ge(qk_done, at(qk_done, l, 3))
                        for i in range(2):
                            for t in range(2 * i, 2 * i + 2):
                                for m in range(2):
                                    o = ((t % 2) * 2 + m) * P
                                    mm = pe.transpose(PS[:, 2 + i, o:o + P], kend[:, m, t * P:t * P + P], ident[:, :])
                            mm.then_inc(kt_ready, 1)
                        pe.wait_ge(grow_done, at(grow_done, l, 1))
                    channel_major((6 + h) % 8, W_R, slice(h * P, h * P + P)).then_inc(r_ready, 1)

                pe.wait_ge(const_loaded, 16 * 9)
                pe.wait_ge(kt_done, at(kt_done, l, 2))
                pe.wait_ge(r_done, at(r_done, l, GH))
                for m in range(2):
                    for r in range(2):
                        for n in range(r, NCH - 1, 2):
                            for h in range(2):
                                rows = slice(CHUNK * r, CHUNK * r + CHUNK)
                                mm = pe.matmul(PS[HD * h:HD * h + HD, 4 + 2 * m + r, (n // 2) * P:(n // 2) * P + P],
                                               kend_tm[rows, n // 2, m * P + HD * h:m * P + HD * h + HD],
                                               v[rows, n // 2, (2 * m + h) * P:(2 * m + h) * P + P], start=True, stop=True,
                                               skip_group_check=True)
                        mm.then_inc(kv_ready, 1)
                for h in range(GH):
                    rows = slice(HD * (h % 2), HD * (h % 2) + HD)
                    for t in range(NT):
                        mm = pe.matmul(PS[:, h, t * P:t * P + P], kinv[rows, h // 2, t * P:t * P + P],
                                       qdec[rows, h // 2, t * P:t * P + P], start=True, stop=True)
                    mm.then_inc(att_ready, 1)
                for h in range(GH):
                    rows = slice(HD * (h % 2), HD * (h % 2) + HD)
                    pe.wait_ge(att_done, at(att_done, l, h + 1))
                    pe.wait_ge(s_done, at(s_done, l, 1))
                    for t in range(NT):
                        pe.matmul(PS[:, 4 + h, t * P:t * P + P], v[:, t, h * P:h * P + P], attm[:, h % 2, t, :],
                                  start=(t == 0), stop=False, skip_group_check=True)
                    for n in range(1, NCH):
                        mm = pe.matmul(PS[:, 4 + h, n * CHUNK:n * CHUNK + CHUNK], S[rows, h // 2, n, :],
                                       qdec[rows, h // 2, n * CHUNK:n * CHUNK + CHUNK], start=False, stop=(n == NCH - 1),
                                       skip_group_check=True)
                    mm.then_inc(o_ready, 1)
                for h in range(GH):
                    pe.wait_ge(osq_done, at(osq_done, l, h + 1))
                    pe.matmul(PS[:, h, :], ones[:, :], osq[h], start=True, stop=True).then_inc(ms_ready, 1)

                pe.wait_ge(rope_done, at(rope_done, l, 1))
                for t in range(NT):
                    pe.wait_ge(orr_done, at(orr_done, l, t + 1))
                    for a in range(QH // 2):
                        mm = pe.transpose(PS[:, t, a * P:a * P + P], qk[:, t, 2 * a:2 * a + 2, :].rearrange("p h d -> p (h d)"), ident[:, :])
                    mm.then_inc(qT_ready, 1)
                for t in range(NT):
                    pe.wait_ge(o_done, at(o_done, l, t + 1))
                    for g in range(KVH):
                        mm = pe.transpose(PS[:, 4 + t, g * P:g * P + P], kd[:, t, g, :, :].rearrange("p r d -> p (r d)"), ident[:, :])
                    mm.then_inc(kT_ready, 1)
                pe.wait_ge(qT_done, at(qT_done, l, NT))
                pe.wait_ge(kT_done, at(kT_done, l, NT))

                def scores(n):
                    if n >= 1:
                        pe.wait_ge(sc_read, at(sc_read, l, n))
                    lo = P if n == 0 else 0
                    for j in range(QH):
                        g, s, a = j // 4, (j % 4) // 2, j % 2
                        rows = slice(HD * s, HD * s + HD)
                        mm = pe.matmul(PS[:, j // 2, 2 * P * a + lo:2 * P * a + 2 * P], qT[rows, 2 * g + a, n * P:n * P + P],
                                       kT[rows, g, (n - 1) * P + lo:(n + 1) * P], start=True, stop=True)
                    mm.then_inc(sc_ready, 1)

                scores(0)
                for n in range(NT):
                    if n + 1 < NT:
                        scores(n + 1)
                    if n == 0:
                        wait_unit(W_MA0)
                    else:
                        pe.wait_ge(early_done, at(early_done, l, n))
                    channel_major(5, W_MA0, slice(n * P, n * P + P)).then_inc(mx_ready, 1)
                    pe.wait_ge(p_done, at(p_done, l, n + 1))
                    first = 1 if n == 0 else 0
                    for b in range(first, 2):
                        i = 2 * n + b - 1
                        if i >= 1:
                            pe.wait_ge(pTa_done, at(pTa_done, l, i))
                        for j in range(4):
                            mm = pe.transpose(PS[:, 4, j * P:j * P + P], sc[n % 2][:, j, b * P:b * P + P], ident[:, :])
                        mm.then_inc(pTa_ready, 1)
                        if i >= 1:
                            pe.wait_ge(pTd_done, at(pTd_done, l, i))
                        for j in range(4):
                            mm = pe.transpose(PS[:, 6, j * P:j * P + P], sc[n % 2][:, 4 + j, b * P:b * P + P], ident[:, :])
                        mm.then_inc(pTd_ready, 1)
                    pe.wait_ge(pTa_done, at(pTa_done, l, 2 * n + 1))
                    pe.wait_ge(pTd_done, at(pTd_done, l, 2 * n + 1))
                    if n >= 1:
                        pe.wait_ge(pv_done, at(pv_done, l, n))
                    for j in range(QH):
                        g, s, a = j // 4, (j % 4) // 2, j % 2
                        for b in range(first, 2):
                            mm = pe.matmul(PS[HD * s:HD * s + HD, 7, (2 * g + a) * P:(2 * g + a) * P + P],
                                           v_tm[:, n - 1 + b, g * HD:g * HD + HD], pT[:, b, j, :],
                                           start=(g == 0 and a == 0 and b == first), stop=(b == 1), skip_group_check=True)
                    mm.then_inc(pv_ready, 1)

                pe.wait_ge(pv_done, at(pv_done, l, NT))
                wait_unit(W_MA1)
                for j in range(C // 2, C):
                    channel_major(j, W_MA1, slice((j % 4) * P, (j % 4) * P + P)).then_inc(mx_ready, 1)
                wait_unit(W_UPG)
                pe.wait_ge(rs_lo, at(rs_lo, l, 1))
                for j in range(C):
                    pe.wait_ge(mx_sig, at(mx_sig, l, j + 1))
                    channel_major(j, W_UPG, slice(j * P, j * P + P), rs_parts).then_inc(mx_ready, 1)
                for j in range(C):
                    if j % 4 == 0:
                        wait_unit(W_MB0 + j // 4)
                    pe.wait_ge(mg_done, at(mg_done, l, j + 1))
                    channel_major(j, W_MB0 + j // 4, slice((j % 4) * P, (j % 4) * P + P)).then_inc(mx_ready, 1)
                wait_unit(W_UPS)
                pe.wait_ge(os_lo, at(os_lo, l, 1))
                for j in range(C):
                    pe.wait_ge(mx_sig, at(mx_sig, l, C + j + 1))
                    channel_major(j, W_UPS, slice(j * P, j * P + P), os_parts).then_inc(mx_ready, 1)
                for i in range(2 * NT):
                    t, n = i % NT, W_O0 + i // NT
                    if t == 0:
                        wait_unit(n)
                    token_major(i, t, n, 512, mT_parts, m_lo if i == 0 else None).then_inc(out_ready, 1)

                pe.wait_ge(x_done, at(x_done, l, 2 * NT))
                pe.wait_ge(xs_ready, at(xs_ready, l, 2 * NT))
                transpose_tokens(range(C))
                for k in range(C):
                    pe.wait_ge(ht_done, at(ht_done, l, C + k + 1))
                    mm = pe.matmul(PS[0:E, 0, :], wr[:, k, :], hT[:, k, :], start=(k == 0), stop=(k == C - 1))
                mm.then_inc(lgT_ready, 1)
                pe.wait_ge(const_loaded, 16 * 9)
                pe.wait_ge(lgT_done, at(lgT_done, l, 1))
                for t in range(NT):
                    mm = pe.transpose(PS[:, 1, t * E:t * E + E], lgT[:, t * P:t * P + P], ident[0:E, 0:E])
                mm.then_inc(lg_ready, 1)
                gate_rows(1, 3)
                pe.wait_ge(m_done, at(m_done, l, 1))
                pe.matmul(PS[:, 1, 0:NT * E], before[:, :], rt[:, MASK, :], start=True, stop=True)
                pe.matmul(PS[:, 1, NT * E:2 * NT * E], ones[:, :], rt[:, MASK, :], start=True, stop=True).then_inc(rk_ready, 1)
                pe.wait_ge(row_done, at(row_done, l, 1))
                pe.wait_ge(grow_done, at(grow_done, l, 2))

                def tokens(src, raise_at_first=None):
                    for k in range(C):
                        mm = pe.transpose(PS[:, 2 + k // 4, (k % 4) * P:(k % 4) * P + P], src[:, k * P:k * P + P], ident[:, :])
                        if k == 0 and raise_at_first is not None:
                            mm.then_inc(raise_at_first, 1)
                    return mm

                def up_product(bank, k, part):
                    w = (gu_high[part].rearrange("p (c n) -> p c n", c=C), chunks(ring_r[:, 3 * k + part, :], C))
                    for c_ in range(C):
                        mm = three_passes(PS[:, bank, :], [a[:, c_, :] for a in xgT_parts], [a[:, c_, :] for a in w],
                                          c_ == 0, c_ == C - 1)
                    return mm

                def hidden(src, raise_at_first=None):
                    for f in range(FC):
                        mm = pe.transpose(PS[:, 4, f * P:f * P + P], src[:, f * P:f * P + P], ident[:, :])
                        if f == 0 and raise_at_first is not None:
                            mm.then_inc(raise_at_first, 1)
                    return mm

                def down_product(aT_, w):
                    for h in range(2):
                        for f in range(FC):
                            mm = pe.matmul(PS[:, 5 + h, :], aT_[:, f, :], w[:, f, 512 * h:512 * h + 512], start=(f == 0), stop=(f == FC - 1))
                    return mm

                def weights(k, part):
                    return slot(3 * k + part, (C, C, FC)[part])

                def wait_weights(pair, k, part):
                    s = loaded[3 * k + part]
                    pe.wait_ge(s, at(s, l, 16 * (BEFORE_MOE[3 * k + part] + 1) + 16 * pair))

                def gate_up(e, pair, k):
                    pe.wait_ge(x_lo, at(x_lo, l, e + 1))
                    pe.wait_ge(gu_lo[0], at(gu_lo[0], l, 2 * e + 2))
                    up_product(0, k, 0).then_inc(g_ready, 1)
                    pe.wait_ge(gu_lo[1], at(gu_lo[1], l, 2 * e + 2))
                    up_product(1, k, 1).then_inc(u2_ready, 1)

                def transposed_tokens(e, pair, k, raise_at_first=None):
                    pe.wait_ge(xg_loaded[k], at(xg_loaded[k], l, 16 * pair + 16))
                    tokens(xg[k], raise_at_first).then_inc(t1_ready, 1)

                def finish_a(e, k):
                    pe.wait_ge(act_done, at(act_done, l, e + 1))
                    hidden(mact[k], gu_free).then_inc(t2_ready, 1)

                def finish_b(e, pair, k):
                    pe.wait_ge(t2_done, at(t2_done, l, e + 1))
                    wait_weights(pair, k, 2)
                    pe.wait_ge(y_done, at(y_done, l, e + 1))
                    down_product(maT[k], weights(k, 2)).then_inc(d_ready, 1)

                def overflow(e, pair, k, y_before):
                    def body(b, n):
                        pe.wait_ge(o_gath, 16 * n)
                        tokens(o_xg).then_inc(o_t1, 1)
                        pe.wait_ge(act_done, at(act_done, l, e + 1))
                        pe.wait_ge(o_xl, n)
                        up_product(0, k, 0)
                        up_product(1, k, 1).then_inc(o_gu, 1)
                        pe.wait_ge(o_ac, n)
                        hidden(o_act).then_inc(o_t2, 1)
                        pe.wait_ge(o_t2c, n)
                        wait_weights(pair, k, 2)
                        pe.wait_ge(y_done, at(y_done, l, y_before))
                        down_product(o_aT, weights(k, 2)).then_inc(o_d, 1)
                        pe.wait_ge(o_y, n)
                    overflow_blocks(pe, e, done, body)

                transposed_tokens(0, 0, 0)
                gate_up(0, 0, 0)
                overflow(0, 0, 0, 1)
                transposed_tokens(1, 0, 1, gu_free)

                def step(s, pair, k, pair_before, more=True):
                    pe.wait_ge(act_done, at(act_done, l, s))
                    gate_up(s, pair, k)
                    overflow(s, pair, k, s)
                    finish_a(s - 1, 1 - k)
                    if more:
                        transposed_tokens(s + 1, pair + k, 1 - k)
                    finish_b(s - 1, pair_before, 1 - k)

                with pe.Fori(0, E // 2 - 1) as j:
                    step(2 * j + 1, j, 1, j)
                    step(2 * j + 2, j + 1, 0, j)
                step(E - 1, E // 2 - 1, 1, E // 2 - 1, more=False)
                pe.wait_ge(act_done, at(act_done, l, E))
                hidden(mact[1]).then_inc(t2_ready, 1)
                finish_b(E - 1, E // 2 - 1, 1)
                with pe.If(l < DEPTH - 1):
                    for u in range(ADA_EARLY):
                        condition_products(l + 1, [u])
                        condition_sums(l + 1, [u])
                    pe.nop()

        @block.vector
        def _(dve):
            tt, ts, stt = dve.tensor_tensor, dve.tensor_scalar, dve.scalar_tensor_tensor
            done = dve.alloc_register("dve_ovf")
            dve.reg_mov(done, 0)
            dve.memset(cst[:, 0:1], EPS)
            dve.memset(cst[:, 1:2], 1.0)
            dve.memset(cst[:, 2:3], 0.0).then_inc(dve_consts, 1)
            dve.wait_ge(const_loaded, 16 * 9)
            pf = rt[:, 0, 0:NT]
            ang = rt[:, 1, 0:NT * HALF].rearrange("p (t i) -> p t i", t=NT)
            turn = rt[:, 2, 0:NT * HALF].rearrange("p (t i) -> p t i", t=NT)
            dve.tensor_copy(pf, posi[:, :])
            dve.drain()
            freq = np.power(np.float32(ROPE_THETA), -np.arange(HALF, dtype=np.float32) / np.float32(HALF))
            for i in range(HALF):
                ts(ang[:, :, i:i + 1], pf.unsqueeze(2), float(freq[i]), None, ALU.mult)
            dve.drain()
            round_to = 1.5 * 2.0 ** 23
            ts(turn, ang, float(1 / (2 * np.pi)), round_to, ALU.mult, ALU.add)
            dve.drain()
            ts(turn, turn, -round_to, None, ALU.add)
            dve.drain()
            two_pi_hi = 6.28125
            mid = np.float32(2 * np.pi - two_pi_hi)
            mid = float((mid.view(np.uint32) & np.uint32(0xFFFFF000)).view(np.float32))
            for part in (two_pi_hi, mid, float(2 * np.pi - two_pi_hi - mid)):
                stt(ang, turn, -part, ang, ALU.mult, ALU.add)
                dve.drain()
            ts(sinr[:, :, :], ang, -3.1415925, 3.1415925, ALU.max, ALU.min)
            dve.drain()
            ts(turn, sinr[:, :, :], -1.0, None, ALU.mult)
            dve.drain()
            tt(turn, turn, sinr[:, :, :], ALU.max)
            dve.drain()
            ts(cosr[:, :, :], turn, -1.0, float(np.pi / 2), ALU.mult, ALU.add).then_inc(trig, 1)
            dve.wait_ge(cond_sig, 1)
            tt(condT[:, :], PS[:, 2, 0:C], a1[:, :], ALU.mult).then_inc(cond_done, 1)
            dve.wait_ge(pcs_ready, 1)
            dve.tensor_copy(pcs[:, :, :].rearrange("p l n -> p (l n)"), PS[:, 3, 0:DEPTH * R_END])

            def condition(l, units):
                for u in units:
                    dve.wait_ge(loaded[u % SLOTS], at(loaded[u % SLOTS], l, 16 * (u // SLOTS + 1)))
                    if u >= 2:
                        dve.wait_ge(ada_summed, at(ada_summed, l, u - 1))
                    acc = ada_acc[u % 2]
                    product = ts(acc, slot(u)[:, 0, :], condT[:, 0:1], None, ALU.mult)
                    for k in range(1, ADA_DVE):
                        dve.drain()
                        product = stt(acc, slot(u)[:, k, :], condT[:, k:k + 1], acc, ALU.mult, ALU.add)
                    product.then_inc(ada_ready, 1)

            dve.drain()
            condition(0, range(ADA_EARLY))
            dve.wait_ge(pool_consts, 14)
            dve.wait_ge(x_loaded, 16)
            dve.wait_ge(trig_act, 1)
            with dve.Fori(0, DEPTH) as l:
                def norm_tokens(r):
                    dve.wait_ge(root, at(root, l, r + 1))
                    dve.reciprocal(rstd[:, :], ss[:, :])
                    dve.drain()
                    for t in range(NT):
                        ts(xs[:, t, :], xt[:, t, :], rstd[:, t:t + 1], None, ALU.mult).then_inc(xs_ready, 1)

                def gate_diagonal(row):
                    tt(diag, ident[:, :].unsqueeze(1).broadcast_to([P, C, P]),
                       pc[:, row:row + C].unsqueeze(2).broadcast_to([P, C, P]), ALU.mult).then_inc(diag_done, 1)

                condition(l, [ADA_EARLY])
                norm_tokens(0)
                condition(l, range(ADA_EARLY + 1, ADA))
                dve.memset(attm[:, :, :, :], 0.0)
                dve.wait_ge(ada_summed, at(ada_summed, l, ADA))
                tt(pc[:, 0:R_NM], PS[:, 7, 0:R_NM], pcs[:, bass.ds(l, 1), 0:R_NM].rearrange("p a n -> p (a n)"), ALU.add)
                ts(pc[:, R_NM:], pcs[:, bass.ds(l, 1), R_NM:].rearrange("p a n -> p (a n)"), 1.0, None, ALU.mult)
                dve.drain()
                stt(a1[:, :], pc[:, R_SC1:R_SC1 + C], 1.0, pc[:, R_NM:R_NM + C], ALU.add, ALU.mult)
                stt(a2[:, :], pc[:, R_SC2:R_SC2 + C], 1.0, pc[:, R_NF:R_NF + C], ALU.add, ALU.mult)
                gate_diagonal(R_G1)

                def split_low(n):
                    for h in range(2):
                        cols = slice(half_split[n] * h, half_split[n] * (h + 1))
                        w = ring[:, unit_slot(n), cols]
                        dve.wait_ge(hi_done, at(hi_done, l, 2 * n + h + 1))
                        tt(ring_r[:, unit_slot(n), cols], w, ring_r[:, 2 + n % 2, cols].bitcast(F32), ALU.subtract).then_inc(lo_done, 1)

                split_low(0)
                split_low(1)
                for k in range(C):
                    dve.wait_ge(ht_done, at(ht_done, l, k + 1))
                    dve.wait_ge(a_part, at(a_part, l, k + 1))
                    tt(hT_parts[1][:, k, :], hT[:, k, :], hT_parts[0][:, k, :].bitcast(F32), ALU.subtract).then_inc(hx_lo, 1)
                split_low(2)

                for i in range(2):
                    dve.wait_ge(qsq_done, at(qsq_done, l, i + 1))
                    dve.tensor_reduce(qss[:, 2 * i:2 * i + 2, :], sqt.rearrange("p (t h d) -> p t h d", t=2, h=NN), AX.X, ALU.add).then_inc(qss_done, 1)
                split_low(3)
                dve.wait_ge(qrt_done, at(qrt_done, l, 1))
                dve.reciprocal(qss[:, :, :], qss[:, :, :])
                dve.drain()
                heads = qk.rearrange("p t h d -> p (t h) d")
                tt(heads, heads, qss[:, :, :].rearrange("p t h -> p (t h)").unsqueeze(2).broadcast_to([P, NT * NN, HD]), ALU.mult)
                dve.drain()
                dve.wait_ge(par_loaded, at(par_loaded, l, 16 * 4))
                for part, hs in enumerate((slice(0, QH), slice(QH, NN))):
                    tt(qk[:, :, hs, :], qk[:, :, hs, :],
                       gains[:, part:part + 1, :].unsqueeze(1).broadcast_to([P, NT, hs.stop - hs.start, HD]), ALU.mult)
                dve.drain()
                x1, x2 = qk[:, :, :, 0:HALF], qk[:, :, :, HALF:2 * HALF]
                w = NT * NN * HALF
                tmp = [sqt[:, w * i:w * i + w].rearrange("p (t h i) -> p t h i", t=NT, h=NN) for i in range(4)]
                cos = cosr[:, :, :].unsqueeze(2).broadcast_to([P, NT, NN, HALF])
                sin = sinr[:, :, :].unsqueeze(2).broadcast_to([P, NT, NN, HALF])
                tt(tmp[0], x1, cos, ALU.mult)
                tt(tmp[1], x2, sin, ALU.mult)
                tt(tmp[2], x2, cos, ALU.mult)
                tt(tmp[3], x1, sin, ALU.mult)
                dve.drain()
                tt(x1, tmp[0], tmp[1], ALU.subtract)
                tt(x2, tmp[2], tmp[3], ALU.add)
                dve.drain()
                split_low(4)

                dve.wait_ge(labs, at(labs, l, 1))
                ts(la, la, 0.0, None, ALU.min)
                dve.drain()
                dve.wait_ge(lln, at(lln, l, 1))
                tt(la, la, bb, ALU.subtract)
                dve.drain()
                dve.wait_ge(scanm_made, at(scanm_made, l, 2))
                for m in range(2):
                    scan = dve.tensor_tensor_scan(bb[:, m, :], scanm, la[:, m, :], 0.0, ALU.mult, ALU.add)
                scan.then_inc(b_done, 1)
                dve.drain()
                per_chunk = bb.rearrange("p m (n s) -> p (m n) s", s=CHUNK)
                tt(la.rearrange("p m (n s) -> p (m n) s", s=CHUNK), per_chunk,
                   per_chunk[:, :, CHUNK - 1:CHUNK].broadcast_to([P, 2 * NCH, CHUNK]), ALU.subtract).then_inc(dif_done, 1)
                dve.wait_ge(eplus, at(eplus, l, 1))
                dve.wait_ge(qk_ready, at(qk_ready, l, 2))
                stt(qdec, PS[:, 2:4, :], float(HD) ** -0.5, qdec, ALU.mult, ALU.mult).then_inc(qk_done, 1)
                dve.wait_ge(qk_ready, at(qk_ready, l, 4))
                tt(kinv, PS[:, 4:6, :], kinv, ALU.mult).then_inc(qk_done, 1)
                dve.wait_ge(eend, at(eend, l, 1))
                tt(kend, PS[:, 4:6, :], kend, ALU.mult).then_inc(qk_done, 1)
                split_low(5)
                for h in range(GH):
                    dve.wait_ge(r_sig, at(r_sig, l, h + 1))
                    stt(rs[:, h, :], PS[:, (6 + h) % 8, :], pc[:, R_GN + h:R_GN + h + 1], rs[:, h, :], ALU.mult, ALU.mult).then_inc(r_done, 1)
                    if h == 1:
                        for i in range(2):
                            dve.wait_ge(kt_ready, at(kt_ready, l, i + 1))
                            dve.tensor_copy(kend_tm[:, 2 * i:2 * i + 2, :], PS[:, 2 + i, :].rearrange("p (t n) -> p t n", t=2)).then_inc(kt_done, 1)

                def mask_scores(h):
                    dve.wait_ge(x_loaded, 16)
                    dve.wait_ge(att_ready, at(att_ready, l, h + 1))
                    if h >= 2:
                        dve.wait_ge(o_ready, at(o_ready, l, h - 1))
                    dve.copy_predicated(attm[:, h % 2, :, :], causal[:, :].bitcast(U32).unsqueeze(1).broadcast_to([P, NT, P]),
                                        PS[:, h, :].rearrange("p (t s) -> p t s", t=NT)).then_inc(att_done, 1)

                dve.wait_ge(kv_ready, at(kv_ready, l, 4))
                for m in range(2):
                    dve.tensor_copy(S[:, m, 1, :], PS[:, 4 + 2 * m, 0:P])
                for n in range(1, NCH - 1):
                    dve.drain()
                    for m in range(2):
                        step = stt(S[:, m, n + 1, :], S[:, m, n, :], decay[:, m, n:n + 1],
                                   PS[:, 4 + 2 * m + n % 2, (n // 2) * P:(n // 2) * P + P], ALU.mult, ALU.add)
                step.then_inc(s_done, 1)
                for h in range(GH):
                    mask_scores(h)
                for r in range(2):
                    cp = dve.tensor_copy(kd[:, :, :, r, :], qk[:, :, QH:NN, :])
                cp.then_inc(rope_done, 1)
                for h in range(GH):
                    dve.wait_ge(osq_done, at(osq_done, l, h + 1))
                    tt(rs[:, h, :], PS[:, 4 + h, :], rs[:, h, :], ALU.mult)
                for h in range(GH):
                    dve.wait_ge(orr_done, at(orr_done, l, h + 1))
                    root_ = orr[h % 2]
                    dve.reciprocal(root_, root_)
                    dve.drain()
                    tt(rs[:, h, :], root_, rs[:, h, :], ALU.mult).then_inc(o_done, 1)

                for t in range(NT):
                    dve.wait_ge(kT_ready, at(kT_ready, l, t + 1))
                    dve.tensor_copy(kT[:, :, t * P:t * P + P], PS[:, 4 + t, 0:2 * P].rearrange("p (g s) -> p g s", g=KVH)).then_inc(kT_done, 1)

                sink_j = sink_t[:, :].rearrange("p (g a s) -> p g s a", g=KVH, s=2)

                def by_head(tile):
                    return tile.rearrange("p (g s a) -> p g s a", g=KVH, s=2)

                def score_max(n):
                    lo = P if n == 0 else 0
                    if n >= 2:
                        dve.wait_ge(pTa_ready, at(pTa_ready, l, 2 * n - 3))
                        dve.wait_ge(pTd_ready, at(pTd_ready, l, 2 * n - 3))
                    dve.wait_ge(sc_ready, at(sc_ready, l, n + 1))
                    stt(sc[n % 2][:, :, lo:], PS[:, 0:4, :].rearrange("p b (a s) -> p (b a) s", a=2)[:, :, lo:], float(HD) ** -0.5,
                        band[:, lo:].unsqueeze(1).broadcast_to([P, QH, 2 * P - lo]), ALU.mult, ALU.add).then_inc(sc_read, 1)
                    dve.drain()
                    dve.tensor_reduce(smax[:, :], sc[n % 2][:, :, lo:], AX.X, ALU.max)
                    dve.drain()
                    tt(by_head(smax[:, :]), by_head(smax[:, :]), sink_j, ALU.max)
                    dve.drain()
                    ts(nmax[:, n % 2, :], smax[:, :], -1.0, None, ALU.mult)
                    tt(by_head(snk[:, n % 2, :]), sink_j, by_head(smax[:, :]), ALU.subtract).then_inc(max_done, 1)

                score_max(0)
                for n in range(NT):
                    lo = P if n == 0 else 0
                    if n + 1 < NT:
                        score_max(n + 1)
                    dve.wait_ge(p_exp, at(p_exp, l, n + 1))
                    tt(ssum[:, n % 2, :], ssum[:, n % 2, :], snk[:, n % 2, :], ALU.add)
                    dve.drain()
                    dve.reciprocal(ssum[:, n % 2, :], ssum[:, n % 2, :])
                    dve.drain()
                    tt(sc[n % 2][:, :, lo:], sc[n % 2][:, :, lo:], ssum[:, n % 2, :].unsqueeze(2).broadcast_to([P, QH, 2 * P - lo]),
                       ALU.mult).then_inc(p_done, 1)
                    for b in range(1 if n == 0 else 0, 2):
                        dve.wait_ge(pTd_ready, at(pTd_ready, l, 2 * n + b))
                        dve.tensor_copy(pT[:, b, 4:8, :], PS[:, 6, :].rearrange("p (j s) -> p j s", s=P)).then_inc(pTd_done, 1)

                split_low(W_MA1)
                dve.wait_ge(rs_hi, at(rs_hi, l, 1))
                tt(rs_parts[1].rearrange("p h s -> p (h s)"), reg4[:, :], rs_parts[0].rearrange("p h s -> p (h s)").bitcast(F32),
                   ALU.subtract).then_inc(rs_lo, 1)
                split_low(W_UPG)
                for j in range(C):
                    dve.wait_ge(mx_sig, at(mx_sig, l, j + 1))
                    dve.wait_ge(mx_ready, at(mx_ready, l, C + j + 1))
                    tt(mT[:, j, :], PS[:, j, :], mT[:, j, :], ALU.mult).then_inc(mg_done, 1)
                    if j == C // 2 - 1:
                        split_low(W_MB0)
                dve.wait_ge(os_hi, at(os_hi, l, 1))
                tt(os_parts[1].rearrange("p h s -> p (h s)"), reg0[:, 2048:4096],
                   os_parts[0].rearrange("p h s -> p (h s)").bitcast(F32), ALU.subtract).then_inc(os_lo, 1)
                split_low(W_MB1)
                split_low(W_UPS)
                split_low(W_O0)
                def merged_low(j):
                    dve.wait_ge(m_hi, at(m_hi, l, j + 1))
                    tt(mT_parts[1][:, j, :], mT[:, j, :], mT_parts[0][:, j, :].bitcast(F32), ALU.subtract).then_inc(m_lo, 1)

                for j in range(C):
                    gated = sigb[j // 4][:, j % 4, :]
                    dve.wait_ge(mx_sig, at(mx_sig, l, C + j + 1))
                    dve.wait_ge(mx_ready, at(mx_ready, l, 3 * C + j + 1))
                    tt(gated, PS[:, j, :], gated, ALU.mult)
                    dve.drain()
                    tt(mT[:, j, :], mT[:, j, :], gated, ALU.add).then_inc(mx_done, 1)
                    if j >= 1:
                        merged_low(j - 1)
                merged_low(C - 1)
                split_low(W_O1)
                dve.wait_ge(grow_done, at(grow_done, l, 1))
                for i in range(2 * NT):
                    t, cols = i % NT, slice(512 * (i // NT), 512 * (i // NT) + 512)
                    dve.wait_ge(out_ready, at(out_ready, l, i + 1))
                    tt(otmp[i % 2], PS[:, i, :], grow[:, cols], ALU.mult)
                    dve.drain()
                    tt(xt[:, t, cols], xt[:, t, cols], otmp[i % 2], ALU.add).then_inc(x_done, 1)
                gate_diagonal(R_G2)
                norm_tokens(1)

                dve.wait_ge(aff_done, at(aff_done, l, 1))
                aff, sel, key = rt[:, 0, :], rt[:, 1, :], rt[:, 2, :]
                tt(sel.rearrange("p (t e) -> p t e", e=E), aff.rearrange("p (t e) -> p t e", e=E),
                   br[:, :].unsqueeze(1).broadcast_to([P, NT, E]), ALU.add)
                dve.drain()
                four = sel.rearrange("p (q a b) -> p q a b", a=2, b=2)
                hi2 = rt[:, 3, 0:2 * NT * G4].rearrange("p (q a) -> p q a", a=2)
                lo2 = rt[:, 4, 0:2 * NT * G4].rearrange("p (q a) -> p q a", a=2)
                tt(hi2, four[:, :, :, 0], four[:, :, :, 1], ALU.max)
                tt(lo2, four[:, :, :, 0], four[:, :, :, 1], ALU.min)
                dve.drain()
                q = NT * G4
                top1, top2, low = rt[:, 5, 0:q], rt[:, 6, 0:q], rt[:, 7, 0:q]
                tt(top1, hi2[:, :, 0], hi2[:, :, 1], ALU.max)
                tt(top2, hi2[:, :, 0], hi2[:, :, 1], ALU.min)
                tt(low, lo2[:, :, 0], lo2[:, :, 1], ALU.max)
                dve.drain()
                tt(top2, top2, low, ALU.max)
                dve.drain()
                tt(top1, top1, top2, ALU.add)
                dve.drain()

                def first_max(score, n, weight, hot, small, keys):
                    rows = score.rearrange("p (t n) -> p t n", n=n)
                    keys, hot = (a.rearrange("p (t n) -> p t n", n=n) for a in (keys, hot))
                    dve.tensor_reduce(small, rows, AX.X, ALU.max)
                    dve.drain()
                    tt(keys, rows, small.unsqueeze(2).broadcast_to([P, NT, n]), ALU.is_equal)
                    dve.drain()
                    tt(keys, keys, weight[:, :].unsqueeze(1).broadcast_to([P, NT, n]), ALU.mult)
                    dve.drain()
                    dve.tensor_reduce(small, keys, AX.X, ALU.max)
                    dve.drain()
                    tt(hot, keys, small.unsqueeze(2).broadcast_to([P, NT, n]), ALU.is_equal)
                    dve.drain()

                small = rt[:, 8, 0:NT]
                group, off = rt[:, 9, 0:q], rt[:, 10, 0:q]
                first_max(top1, G4, wg4, group, small, key[:, 0:q])
                ts(off, group, -1.0, -NEG, ALU.add, ALU.mult)
                tt(sel.rearrange("p (q e) -> p q e", e=G4), sel.rearrange("p (q e) -> p q e", e=G4),
                   group.unsqueeze(2).broadcast_to([P, q, G4]), ALU.mult)
                dve.drain()
                tt(sel.rearrange("p (q e) -> p q e", e=G4), sel.rearrange("p (q e) -> p q e", e=G4),
                   off.unsqueeze(2).broadcast_to([P, q, G4]), ALU.add)
                dve.drain()
                hot = [rt[:, 11, :], rt[:, 12, :]]
                first_max(sel, E, w16, hot[0], small, key)
                stt(sel, hot[0], 3 * NEG, sel, ALU.mult, ALU.add)
                dve.drain()
                first_max(sel, E, w16, hot[1], small, key)
                tt(rt[:, MASK, :], hot[0], hot[1], ALU.add).then_inc(m_done, 1)
                pair = rt[:, 14, 0:2 * NT].rearrange("p (k t) -> p k t", k=TOPK)
                for k in range(TOPK):
                    tt(key, aff, hot[k], ALU.mult)
                    dve.drain()
                    dve.tensor_reduce(pair[:, k, :], key.rearrange("p (t e) -> p t e", e=E), AX.X, ALU.add)
                    dve.drain()
                tt(small, pair[:, 0, :], pair[:, 1, :], ALU.add)
                dve.drain()
                dve.reciprocal(small, small)
                dve.drain()
                tt(wts[:, :, :], pair, small.unsqueeze(1).broadcast_to([P, TOPK, NT]), ALU.mult)
                dve.wait_ge(rk_ready, at(rk_ready, l, 1))
                rank, per_tile = rt[:, 15, :], rt[:, 16, :]
                dve.tensor_copy(rt[:, 15:17, :].rearrange("p a n -> p (a n)"), PS[:, 1, 0:2 * NT * E])
                dve.drain()
                for t in range(1, NT):
                    tt(per_tile[:, t * E:t * E + E], per_tile[:, t * E:t * E + E], per_tile[:, t * E - E:t * E], ALU.add)
                    dve.drain()
                tt(rank[:, E:], rank[:, E:], per_tile[:, 0:(NT - 1) * E], ALU.add)
                dve.tensor_copy(cnt_i[:, :], per_tile[:, (NT - 1) * E:])
                dve.drain()
                blk, row = rt[:, 17, :], rt[:, 18, :]
                ts(blk, rank, float(P), None, ALU.is_ge)
                dve.drain()
                for b in range(2, NT):
                    stt(blk, rank, float(P * b), blk, ALU.is_ge, ALU.add)
                    dve.drain()
                stt(row.rearrange("p (t e) -> p t e", e=E), blk.rearrange("p (t e) -> p t e", e=E), 1.0 - G4 * E * P,
                    e4[:, :].unsqueeze(1).broadcast_to([P, NT, E]), ALU.mult, ALU.add)
                dve.drain()
                stt(row, rank, float(G4 * E), row, ALU.mult, ALU.add)
                dve.drain()
                rows = rt[:, 19, 0:2 * NT].rearrange("p (k t) -> p k t", k=TOPK)
                for k in range(TOPK):
                    tt(key, row, hot[k], ALU.mult)
                    dve.drain()
                    dve.tensor_reduce(rows[:, k, :], key.rearrange("p (t e) -> p t e", e=E), AX.X, ALU.add)
                    dve.drain()
                dve.tensor_copy(row_i[:, :].rearrange("p (k t) -> p k t", k=TOPK), rows).then_inc(row_done, 1)
                def weights_low(e, k, part):
                    for h in range(2):
                        cols = slice(2048 * h, 2048 * h + 2048)
                        dve.wait_ge(gu_hi[part], at(gu_hi[part], l, 2 * e + h + 1))
                        tt(ring_r[:, 3 * k + part, cols], ring[:, 3 * k + part, cols], gu_high[part][:, cols].bitcast(F32),
                           ALU.subtract).then_inc(gu_lo[part], 1)

                weights_low(0, 0, 0)
                weights_low(0, 0, 1)
                dve.wait_ge(tab_loaded, at(tab_loaded, l, 16))
                ts(gidx[:, :], table[:, :], TOPK * SEQ - 1, None, ALU.min)
                dve.drain()
                ts(gidx[:, :], gidx[:, :], 1, None, ALU.arith_shift_right).then_inc(idx_done, 1)
                dve.drain()
                dve.wait_ge(grow_done, at(grow_done, l, 2))
                dve.tensor_copy(rstd[:, :], rstd[:, :]).then_inc(y_done, 1)

                def act_product(dst, s):
                    tt(dst, PS[:, 0, :], s, ALU.mult)
                    dve.drain()
                    return tt(dst, PS[:, 1, :], dst, ALU.mult)

                def outputs(dst):
                    return tt(dst.rearrange("p (a s) -> p a s", a=2), PS[:, 5:7, :], grow[:, :].rearrange("p (a s) -> p a s", a=2), ALU.mult)

                def hidden(e, k):
                    dve.wait_ge(sig_done, at(sig_done, l, e + 1))
                    dve.wait_ge(u2_ready, at(u2_ready, l, e + 1))
                    act_product(mact[k], msig[k]).then_inc(act_done, 1)

                def finish(e, k):
                    dve.wait_ge(d_ready, at(d_ready, l, e + 1))
                    outputs(ysb[k]).then_inc(y_done, 1)

                def tokens_low():
                    return tt(reg23_r[:, 3072:4096], xgT, xgT_parts[0].rearrange("p c s -> p (c s)").bitcast(F32), ALU.subtract)

                def parts_low(e, k):
                    weights_low(e, k, 0)
                    dve.wait_ge(x_hi, at(x_hi, l, e + 1))
                    tokens_low().then_inc(x_lo, 1)
                    weights_low(e, k, 1)

                def overflow(e):
                    def body(b, n):
                        dve.wait_ge(o_t1c, n)
                        tokens_low().then_inc(o_xl, 1)
                        dve.wait_ge(o_sg, n)
                        act_product(o_act, o_sig).then_inc(o_ac, 1)
                        dve.wait_ge(o_d, n)
                        outputs(o_ysb).then_inc(o_y, 1)
                    overflow_blocks(dve, e, done, body)

                dve.wait_ge(x_hi, at(x_hi, l, 1))
                tokens_low().then_inc(x_lo, 1)
                hidden(0, 0)
                overflow(0)
                parts_low(1, 1)

                def step(s, k, stored, more=True):
                    hidden(s, k)
                    overflow(s)
                    if more:
                        parts_low(s + 1, 1 - k)
                    if stored is not None:
                        dve.wait_ge(y_stored[1 - k], at(y_stored[1 - k], l, 16 * stored))
                    finish(s - 1, 1 - k)

                step(1, 1, None)
                step(2, 0, None)
                with dve.Fori(0, E // 2 - 2) as j:
                    step(2 * j + 3, 1, j + 1)
                    step(2 * j + 4, 0, j + 1)
                step(E - 1, 1, E // 2 - 1, more=False)
                dve.wait_ge(y_stored[1], at(y_stored[1], l, 16 * (E // 2 - 1)))
                finish(E - 1, 1)
                with dve.If(l < DEPTH - 1):
                    condition(l + 1, range(ADA_EARLY))
                    dve.nop()
                for t in range(NT):
                    dve.wait_ge(yc_loaded[t], at(yc_loaded[t], l, 16))
                    for k in range(TOPK):
                        add = stt(xt[:, t, :], yc[t][:, k, :], wts[:, k, t:t + 1], xt[:, t, :], ALU.mult, ALU.add)
                        if k == 0:
                            dve.drain()
                    add.then_inc(x2_done, 1)


_INS = ['x', 'c', 'positions', 'w_ada', 'b_ada', 'norm_mix', 'w_in', 'w_alpha2', 'b_alpha', 'gla_norm', 'q_norm', 'k_norm',
        'sinks', 'w_up_gla', 'w_up_swa', 'w_out', 'norm_ffn', 'w_router', 'b_router', 'w_gate', 'w_up', 'w_down']


def kernel(**inputs):
    import concourse.bacc as bacc
    from concourse.bass_utils import run_bass_kernel_spmd

    nc = bacc.Bacc("TRN2", target_bir_lowering=False, num_devices=1, dynamic_dma_scratch_size=12288)
    arrays, args = {}, []
    for name in _INS:
        a = np.ascontiguousarray(inputs[name])
        arrays["in_" + name] = a
        args.append(nc.dram_tensor("in_" + name, a.shape, mybir.dt.from_np(a.dtype), kind="ExternalInput").ap())
    x = arrays["in_x"]
    args.append(nc.dram_tensor("out_x", x.shape, mybir.dt.from_np(x.dtype), kind="ExternalOutput").ap())
    trunk(nc, *args)
    return run_bass_kernel_spmd(nc, [arrays], core_ids=[0]).results[0]["out_x"]
```
